# Optimizing a Trainium2 kernel written in Bass

```python
import jax
import jax.numpy as jnp
from jax import lax
import numpy as np

D_MODEL = 1024
BATCH = 1
SEQ = 1024
DEPTH = 1

CTX_LEN = 256
GRID_W = 64

DN_HEADS = 4
DN_DK = 128
DN_DV = 128
SSM_HEADS = 8
SSM_P = 64
SSM_N = 128
SSM_G = 2
CHUNK = 64
CONV_K = 3
N_EXPERTS = 16
EC_CAPACITY_FACTOR = 2
D_EXPERT = 512
EPS = 1e-6

DN_QK = DN_HEADS * DN_DK
DN_VW = DN_HEADS * DN_DV
SSM_DI = SSM_HEADS * SSM_P
SSM_BC = SSM_G * SSM_N
D_MIX = DN_VW + SSM_DI
CONV_SPLITS = (DN_QK, DN_QK, DN_VW, SSM_DI, SSM_BC, SSM_BC)
CONV_CH = sum(CONV_SPLITS)
REST_SPLITS = (DN_VW, SSM_DI, 2 * DN_HEADS, 2 * DN_HEADS, 2 * SSM_HEADS)
D_IN_PROJ = CONV_CH + sum(REST_SPLITS)

kernel_name = "hybrid_dit_deltanet_ssd_ecmoe"

def _split(a, sizes):
    return jnp.split(a, np.cumsum(sizes)[:-1].tolist(), axis=-1)

def _rev(a):
    return a[:, ::-1]

def rms_norm(x, g):
    xf = x.astype(jnp.float32)
    y = xf * lax.rsqrt(jnp.mean(xf * xf, axis=-1, keepdims=True) + EPS)
    return (y * g.astype(jnp.float32)).astype(x.dtype)

def l2_normalize(x):
    xf = x.astype(jnp.float32)
    return xf * lax.rsqrt(jnp.sum(xf * xf, axis=-1, keepdims=True) + EPS)

def modulate(h, shift, scale):
    return h * (1.0 + scale) + shift

def conv_grid(u, w, b):
    bsz, t, ch = u.shape
    rows = t // GRID_W
    img = u.reshape(bsz, rows, GRID_W, ch)
    kern = jnp.transpose(w, (1, 2, 0))[:, :, None, :].astype(u.dtype)
    out = lax.conv_general_dilated(img, kern, window_strides=(1, 1), padding="SAME",
                                   dimension_numbers=("NHWC", "HWIO", "NHWC"),
                                   feature_group_count=ch)
    return out.reshape(bsz, t, ch) + b.astype(u.dtype)

def conv_seq(u, w, b):
    taps = w[:, CONV_K // 2, :].astype(u.dtype)
    t = u.shape[1]
    pad = CONV_K // 2
    up = jnp.pad(u, ((0, 0), (pad, pad), (0, 0)))
    out = sum(up[:, i:i + t] * taps[:, i] for i in range(CONV_K))
    return out + b.astype(u.dtype)

def stream_features(h, w_in, conv_w, conv_b, on_grid):
    bsz, t = h.shape[:2]
    proj = jnp.einsum("btd,de->bte", h, w_in)
    conv_in, rest = proj[..., :CONV_CH], proj[..., CONV_CH:]
    conv = conv_grid if on_grid else conv_seq
    u = jax.nn.silu(conv(conv_in, conv_w, conv_b)).astype(jnp.float32)
    q, k, v, xs, bs, cs = _split(u, CONV_SPLITS)
    dn_z, ssm_z, dn_b, dn_a, ssm_dt = _split(rest.astype(jnp.float32), REST_SPLITS)
    return dict(
        q=l2_normalize(q.reshape(bsz, t, DN_HEADS, DN_DK)) * (DN_DK ** -0.5),
        k=l2_normalize(k.reshape(bsz, t, DN_HEADS, DN_DK)),
        v=v.reshape(bsz, t, DN_HEADS, DN_DV),
        x=xs.reshape(bsz, t, SSM_HEADS, SSM_P),
        B=bs.reshape(bsz, t, SSM_G, SSM_N),
        C=cs.reshape(bsz, t, SSM_G, SSM_N),
        dn_z=dn_z,
        ssm_z=ssm_z,
        dn_b=dn_b.reshape(bsz, t, 2, DN_HEADS),
        dn_a=dn_a.reshape(bsz, t, 2, DN_HEADS),
        ssm_dt=ssm_dt.reshape(bsz, t, 2, SSM_HEADS),
    )

def gated_delta_chunked(q, k, v, beta, logg, S0, with_output):
    bsz, t, nh, dk = k.shape
    dv = v.shape[-1]
    nc = t // CHUNK

    def to_chunks(a):
        a = a.reshape(bsz, nc, CHUNK, nh, *a.shape[3:])
        return jnp.moveaxis(a, (1, 3), (0, 2))

    qc, kc, vc, bc, gc = map(to_chunks, (q, k, v, beta, logg))
    G = jnp.cumsum(gc, axis=-1)
    tri = jnp.tril(jnp.ones((CHUNK, CHUNK), dtype=bool))
    strict = jnp.tril(jnp.ones((CHUNK, CHUNK), dtype=bool), -1)
    decay = jnp.where(tri, jnp.exp(jnp.where(tri, G[..., :, None] - G[..., None, :], 0.0)), 0.0)
    kb = kc * bc[..., None]
    lmat = jnp.where(strict, jnp.einsum("cbhid,cbhjd->cbhij", kb, kc) * decay, 0.0)
    rhs = jnp.concatenate([vc * bc[..., None], kb * jnp.exp(G)[..., None]], axis=-1)
    uw = lax.linalg.triangular_solve(lmat + jnp.eye(CHUNK, dtype=lmat.dtype), rhs,
                                     left_side=True, lower=True, unit_diagonal=True)
    u, w = uw[..., :dv], uw[..., dv:]
    g_last = G[..., -1]
    k_tail = kc * jnp.exp(g_last[..., None] - G)[..., None]

    def step(S, inp):
        u_i, w_i, kt_i, gl_i = inp[:4]
        v_new = u_i - jnp.einsum("bhld,bhdv->bhlv", w_i, S)
        if with_output:
            qg_i, qk_i = inp[4:]
            o = jnp.einsum("bhld,bhdv->bhlv", qg_i, S) + jnp.einsum("bhij,bhjv->bhiv", qk_i, v_new)
        else:
            o = None
        S = S * jnp.exp(gl_i)[..., None, None] + jnp.einsum("bhld,bhlv->bhdv", kt_i, v_new)
        return S, o

    xs = (u, w, k_tail, g_last)
    if with_output:
        qk = jnp.where(tri, jnp.einsum("cbhid,cbhjd->cbhij", qc, kc) * decay, 0.0)
        qg = qc * jnp.exp(G)[..., None]
        xs = xs + (qg, qk)
    S_T, o = lax.scan(step, S0, xs)
    if not with_output:
        return None, S_T
    o = jnp.moveaxis(o, (0, 2), (1, 3)).reshape(bsz, t, nh, dv)
    return o, S_T

def ssd_chunked(x, dt, A, Bm, Cm, h0, with_output):
    bsz, t, nh, hp = x.shape
    ng, ns = Bm.shape[2], Bm.shape[3]
    hpg = nh // ng
    nc = t // CHUNK
    xc = jnp.transpose(x.reshape(bsz, nc, CHUNK, ng, hpg, hp), (1, 0, 3, 4, 2, 5))
    dtc = jnp.transpose(dt.reshape(bsz, nc, CHUNK, ng, hpg), (1, 0, 3, 4, 2))
    Bc = jnp.transpose(Bm.reshape(bsz, nc, CHUNK, ng, ns), (1, 0, 3, 2, 4))
    Cc = jnp.transpose(Cm.reshape(bsz, nc, CHUNK, ng, ns), (1, 0, 3, 2, 4))
    Acs = jnp.cumsum(dtc * A.reshape(ng, hpg, 1), axis=-1)
    xdt = xc * dtc[..., None]

    def step(h, inp):
        B_i, C_i, xdt_i, a_i = inp
        a_last = a_i[..., -1:]
        if with_output:
            y_off = jnp.einsum("bgin,bghnp->bghip", C_i, h) * jnp.exp(a_i)[..., None]
        else:
            y_off = None
        st = jnp.einsum("bgjn,bghjp->bghnp", B_i, xdt_i * jnp.exp(a_last - a_i)[..., None])
        h = h * jnp.exp(a_last)[..., None] + st
        return h, y_off

    hT, y_off = lax.scan(step, h0.reshape(bsz, ng, hpg, ns, hp), (Bc, Cc, xdt, Acs))
    hT = hT.reshape(bsz, nh, ns, hp)
    if not with_output:
        return None, hT
    tri = jnp.tril(jnp.ones((CHUNK, CHUNK), dtype=bool))
    decay = jnp.where(tri, jnp.exp(jnp.where(tri, Acs[..., :, None] - Acs[..., None, :], 0.0)), 0.0)
    scores = jnp.einsum("cbgin,cbgjn->cbgij", Cc, Bc)[:, :, :, None] * decay
    y_diag = jnp.einsum("cbghij,cbghjp->cbghip", scores, xdt)
    y = jnp.transpose(y_diag + y_off, (1, 0, 4, 2, 3, 5)).reshape(bsz, t, nh, hp)
    return y, hT

def dn_inputs(f, d, A_log, dt_bias):
    beta = jax.nn.sigmoid(f["dn_b"][:, :, d])
    logg = -jnp.exp(A_log[d]) * jax.nn.softplus(f["dn_a"][:, :, d] + dt_bias[d])
    args = (f["q"], f["k"], f["v"], beta, logg)
    return tuple(_rev(a) for a in args) if d == 1 else args

def ssd_inputs(f, d, A_log, dt_bias):
    dt = jax.nn.softplus(f["ssm_dt"][:, :, d] + dt_bias[d])
    seq_args = (f["x"], dt, f["B"], f["C"])
    if d == 1:
        seq_args = tuple(_rev(a) for a in seq_args)
    x, dt, Bm, Cm = seq_args
    return x, dt, -jnp.exp(A_log[d]).astype(jnp.float32), Bm, Cm

def merge_heads(f, o_dirs, y_dirs, dn_norm_g, ssm_D, ssm_norm_g, w_out, out_dtype):
    o = o_dirs[0] + o_dirs[1]
    bsz, t = o.shape[:2]
    dn = rms_norm(o, dn_norm_g) * jax.nn.silu(f["dn_z"].reshape(o.shape))
    y = y_dirs[0] + y_dirs[1] + ssm_D[:, None] * f["x"]
    yz = y.reshape(bsz, t, SSM_DI) * jax.nn.silu(f["ssm_z"])
    ssm = rms_norm(yz.reshape(bsz, t, SSM_G, SSM_DI // SSM_G),
                   ssm_norm_g.reshape(SSM_G, SSM_DI // SSM_G)).reshape(bsz, t, SSM_DI)
    mixed = jnp.concatenate([dn.reshape(bsz, t, DN_VW), ssm], axis=-1).astype(out_dtype)
    return jnp.einsum("bte,ed->btd", mixed, w_out)

def hybrid_mixer(h_ctx, h_lat, w_in, conv_w, conv_b, dn_A_log, dn_dt_bias, dn_norm_g,
                 ssm_A_log, ssm_dt_bias, ssm_D, ssm_norm_g, w_out, ctx_out):
    fc = stream_features(h_ctx, w_in, conv_w, conv_b, on_grid=False)
    fl = stream_features(h_lat, w_in, conv_w, conv_b, on_grid=True)
    bsz = h_lat.shape[0]
    dn_c, dn_l, ssm_c, ssm_l = [], [], [], []
    for d in range(2):
        unrev = _rev if d == 1 else (lambda a: a)
        S0 = jnp.zeros((bsz, DN_HEADS, DN_DK, DN_DV), jnp.float32)
        o_c, S_c = gated_delta_chunked(*dn_inputs(fc, d, dn_A_log, dn_dt_bias), S0, ctx_out)
        o_l, _ = gated_delta_chunked(*dn_inputs(fl, d, dn_A_log, dn_dt_bias), S_c, True)
        h0 = jnp.zeros((bsz, SSM_HEADS, SSM_N, SSM_P), jnp.float32)
        y_c, H_c = ssd_chunked(*ssd_inputs(fc, d, ssm_A_log, ssm_dt_bias), h0, ctx_out)
        y_l, _ = ssd_chunked(*ssd_inputs(fl, d, ssm_A_log, ssm_dt_bias), H_c, True)
        dn_l.append(unrev(o_l))
        ssm_l.append(unrev(y_l))
        if ctx_out:
            dn_c.append(unrev(o_c))
            ssm_c.append(unrev(y_c))
    m_lat = merge_heads(fl, dn_l, ssm_l, dn_norm_g, ssm_D, ssm_norm_g, w_out, h_lat.dtype)
    m_ctx = merge_heads(fc, dn_c, ssm_c, dn_norm_g, ssm_D, ssm_norm_g, w_out, h_ctx.dtype) if ctx_out else None
    return m_ctx, m_lat

def ec_moe(h, router_w, w_gate, w_up, w_down):
    bsz, t, _ = h.shape
    cap = EC_CAPACITY_FACTOR * t // N_EXPERTS
    aff = jax.nn.softmax(jnp.einsum("btd,de->bte", h, router_w).astype(jnp.float32), axis=-1)
    gate, idx = lax.top_k(jnp.swapaxes(aff, 1, 2), cap)
    bidx = jnp.arange(bsz)[:, None, None]
    xs = h[bidx, idx]
    hid = jax.nn.silu(jnp.einsum("becd,edf->becf", xs, w_gate)) * jnp.einsum("becd,edf->becf", xs, w_up)
    ye = jnp.einsum("becf,efd->becd", hid, w_down) * gate[..., None].astype(h.dtype)
    return jnp.zeros_like(h).at[bidx, idx].add(ye)

def setup_inputs(seed: int = 0) -> dict:
    key = jax.random.key(seed)
    ks = jax.random.split(key, 24)
    f32 = jnp.float32

    def nrm(k, shape, scale):
        return jax.random.normal(k, shape, f32) * scale

    def a_log(k, shape):
        return jnp.log(jax.random.uniform(k, shape, f32, 1.0, 16.0))

    def dt_bias(k, shape):
        dt = jnp.exp(jax.random.uniform(k, shape, f32, float(np.log(1e-3)), float(np.log(1e-1))))
        return dt + jnp.log(-jnp.expm1(-dt))

    return {
        "x": nrm(ks[0], (BATCH, SEQ, D_MODEL), 1.0),
        "c": nrm(ks[1], (BATCH, D_MODEL), 1.0),
        "ctx": nrm(ks[2], (BATCH, CTX_LEN, D_MODEL), 1.0),
        "c_ctx": nrm(ks[3], (D_MODEL,), 1.0),
        "ada_w": nrm(ks[4], (DEPTH, D_MODEL, 6 * D_MODEL), 0.3 * D_MODEL ** -0.5),
        "ada_b": nrm(ks[5], (DEPTH, 6 * D_MODEL), 0.02),
        "norm_g": 1.0 + nrm(ks[6], (DEPTH, 4, D_MODEL), 0.1),
        "w_in": nrm(ks[7], (DEPTH, D_MODEL, D_IN_PROJ), D_MODEL ** -0.5),
        "conv_w": nrm(ks[8], (DEPTH, CONV_CH, CONV_K, CONV_K), 1.0 / CONV_K),
        "conv_b": nrm(ks[9], (DEPTH, CONV_CH), 0.02),
        "dn_A_log": a_log(ks[10], (DEPTH, 2, DN_HEADS)),
        "dn_dt_bias": dt_bias(ks[11], (DEPTH, 2, DN_HEADS)),
        "dn_norm_g": 1.0 + nrm(ks[12], (DEPTH, DN_DV), 0.1),
        "ssm_A_log": a_log(ks[13], (DEPTH, 2, SSM_HEADS)),
        "ssm_dt_bias": dt_bias(ks[14], (DEPTH, 2, SSM_HEADS)),
        "ssm_D": 1.0 + nrm(ks[15], (DEPTH, SSM_HEADS), 0.1),
        "ssm_norm_g": 1.0 + nrm(ks[16], (DEPTH, SSM_DI), 0.1),
        "w_out": nrm(ks[17], (DEPTH, D_MIX, D_MODEL), D_MIX ** -0.5),
        "router_w": nrm(ks[18], (DEPTH, D_MODEL, N_EXPERTS), D_MODEL ** -0.5),
        "exp_w_gate": nrm(ks[19], (DEPTH, N_EXPERTS, D_MODEL, D_EXPERT), D_MODEL ** -0.5),
        "exp_w_up": nrm(ks[20], (DEPTH, N_EXPERTS, D_MODEL, D_EXPERT), D_MODEL ** -0.5),
        "exp_w_down": nrm(ks[21], (DEPTH, N_EXPERTS, D_EXPERT, D_MODEL), D_EXPERT ** -0.5),
    }

def reference(x, c, ctx, c_ctx, ada_w, ada_b, norm_g, w_in, conv_w, conv_b, dn_A_log, dn_dt_bias,
              dn_norm_g, ssm_A_log, ssm_dt_bias, ssm_D, ssm_norm_g, w_out, router_w,
              exp_w_gate, exp_w_up, exp_w_down):
    s_lat = jax.nn.silu(c)
    s_ctx = jax.nn.silu(c_ctx)
    for l in range(DEPTH):
        last = l == DEPTH - 1
        mod_lat = jnp.split((s_lat @ ada_w[l] + ada_b[l])[:, None, :], 6, axis=-1)
        n_ctx_mod = 2 if last else 6
        mod_ctx = jnp.split((s_ctx @ ada_w[l][:, :n_ctx_mod * D_MODEL]
                             + ada_b[l][:n_ctx_mod * D_MODEL])[None, None, :], n_ctx_mod, axis=-1)

        h_lat = modulate(rms_norm(x, norm_g[l, 0]), mod_lat[0], mod_lat[1])
        h_ctx = modulate(rms_norm(ctx, norm_g[l, 0]), mod_ctx[0], mod_ctx[1])
        m_ctx, m_lat = hybrid_mixer(h_ctx, h_lat, w_in[l], conv_w[l], conv_b[l], dn_A_log[l],
                                    dn_dt_bias[l], dn_norm_g[l], ssm_A_log[l], ssm_dt_bias[l],
                                    ssm_D[l], ssm_norm_g[l], w_out[l], ctx_out=not last)
        x = x + mod_lat[2] * rms_norm(m_lat, norm_g[l, 1])

        h_lat = modulate(rms_norm(x, norm_g[l, 2]), mod_lat[3], mod_lat[4])
        y_lat = ec_moe(h_lat, router_w[l], exp_w_gate[l], exp_w_up[l], exp_w_down[l])
        x = x + mod_lat[5] * rms_norm(y_lat, norm_g[l, 3])

        if not last:
            ctx = ctx + mod_ctx[2] * rms_norm(m_ctx, norm_g[l, 1])
            h_ctx = modulate(rms_norm(ctx, norm_g[l, 2]), mod_ctx[3], mod_ctx[4])
            y_ctx = ec_moe(h_ctx, router_w[l], exp_w_gate[l], exp_w_up[l], exp_w_down[l])
            ctx = ctx + mod_ctx[5] * rms_norm(y_ctx, norm_g[l, 3])
    return x


_drawn_inputs = setup_inputs


def setup_inputs(seed=0):
    import zlib

    import numpy as np

    out = dict(_drawn_inputs(seed))
    spreads = {}
    factors = {'ctx': 31.077,
     'c_ctx': 33.638,
     'conv_b': 3.783,
     'dn_A_log': 3.173,
     'dn_norm_g': 3.249,
     'ssm_D': 30.134,
     'ssm_A_log': 3.371,
     'ssm_dt_bias': 2.968,
     'ssm_norm_g': 3.802}
    for name, (base, spread) in spreads.items():
        noise = np.random.default_rng([zlib.crc32(name.encode()), seed]).standard_normal(out[name].shape)
        drawn = base * np.exp(spread * noise) if base else spread * noise
        out[name] = jnp.asarray(drawn.astype(out[name].dtype))
    for name, factor in factors.items():
        out[name] = (out[name] * factor).astype(out[name].dtype)
    return out
```

```python
from contextlib import ExitStack

import concourse.bass as bass
from concourse import mybir

P = 128
F32 = mybir.dt.float32
U32 = mybir.dt.uint32
ALU = mybir.AluOpType
ACT = mybir.ActivationFunctionType
AX = mybir.AxisListType
EPS = 1e-6
NEG = -1.0e30


def hybrid_block(nc, x, c, ctx, c_ctx, ada_w, ada_b, norm_g, w_in, conv_w, conv_b, dn_A_log, dn_dt_bias,
                 dn_norm_g, ssm_A_log, ssm_dt_bias, ssm_D, ssm_norm_g, w_out, router_w,
                 exp_w_gate, exp_w_up, exp_w_down, out):
    T, D = x.shape[1:]
    TC = ctx.shape[1]
    DN_H, DK, SSM_H, SSM_P, SSM_G, GW = 4, 128, 8, 64, 2, 64
    KD = D // P
    NL, NC = T // P, TC // P
    NT = NL + NC
    TA = T + TC
    E_N, F = exp_w_gate.shape[1], exp_w_gate.shape[3]
    KF = F // P
    CAP = 2 * T // E_N
    GR = T // GW
    QK = DN_H * DK
    DI = SSM_H * SSM_P
    CONV_CH = conv_w.shape[1]
    HPG = SSM_H // SSM_G
    OFF_Q, OFF_K, OFF_V, OFF_X = 0, QK, 2 * QK, 3 * QK
    OFF_B, OFF_C = OFF_X + DI, OFF_X + DI + SSM_G * P
    OFF_Z = CONV_CH
    OFF_GATE = OFF_Z + QK + DI
    NGATE = w_in.shape[2] - OFF_GATE
    GD = DN_H + SSM_H
    assert CAP == P and NGATE == 2 * (2 * DN_H + SSM_H) and D == 8 * P and QK == 512 and DI == 512

    z_dram = nc.dram_tensor("z_dram", (NL, P, QK + DI), F32, kind="Internal").ap()
    scan_dram = nc.dram_tensor("scan_dram", (2, NL, P, QK + DI), F32, kind="Internal").ap()
    h2_dram = nc.dram_tensor("h2_dram", (T, D), F32, kind="Internal").ap()
    y_dram = nc.dram_tensor("y_dram", (T, D), F32, kind="Internal").ap()

    with ExitStack() as es:
        def sb(name, shape, dt=F32):
            return es.enter_context(nc.sbuf_tensor(name, shape, dt))

        sems = {}

        def sem(name):
            if name not in sems:
                sems[name] = es.enter_context(nc.semaphore(name))
            return sems[name]

        ident = sb("ident", [P, P])
        ones = sb("ones", [P, P])
        cum_mask = sb("cum_mask", [P, 2, P])
        neg_mask = sb("neg_mask", [P, 2, P])
        lvl_mask = sb("lvl_mask", [P, 2, 7, P])
        NV = 2 * KD + 6 * KD + 4 * KD + CONV_CH // P + 1 + DI // P
        vcols = sb("vcols", [P, NV])
        V_C, V_CC, V_AB, V_NG = 0, KD, 2 * KD, 8 * KD
        V_CB, V_DG, V_SG = 12 * KD, 12 * KD + CONV_CH // P, 12 * KD + CONV_CH // P + 1
        sbc = sb("sbc", [P, 56])
        silu_c = sb("silu_c", [P, KD, 2])
        mods = sb("mods", [P, 6 * KD, 2])
        gain1 = sb("gain1", [P, KD, 2])
        taps = sb("taps", [P, CONV_CH // P, 9])
        rw = sb("rw", [P, KD, E_N])
        ssq = sb("ssq", [P, NT])
        rstd = sb("rstd", [P, NT])
        gates = sb("gates", [P, NT, NGATE])
        beta = sb("beta", [P, NT, 2, DN_H])
        sp = sb("sp", [P, NT, 2, GD])
        ga = sb("ga", [P, NT, 2, GD])
        gb = sb("gb", [P, NT, 2, GD])
        gneg = sb("gneg", [P, 2, GD])
        G = sb("G", [P, NT, 2, GD])
        eG = sb("eG", [P, NT, 2, GD])
        eGt = sb("eGt", [P, NT, 2, GD])
        wtail = sb("wtail", [P, NT, 2, GD])

        arena = sb("arena", [P, 47700])
        at = [0]
        vrows = arena[0:NV, 24000:24000 + P]
        srow = arena[0:1, 24200:24256]

        def take(n):
            at[0] += n
            assert at[0] <= 47700, at[0]
            return arena[:, at[0] - n:at[0]]

        kT = take(DN_H * TA).rearrange("p (h t) -> p h t", h=DN_H)
        qT = take(DN_H * T).rearrange("p (h t) -> p h t", h=DN_H)
        BT = take(SSM_G * TA).rearrange("p (h t) -> p h t", h=SSM_G)
        CT = take(SSM_G * T).rearrange("p (h t) -> p h t", h=SSM_G)
        vtok = take(NT * QK).rearrange("p (t n) -> p t n", t=NT)
        XT0 = at[0]
        xtok = take(NT * DI).rearrange("p (t n) -> p t n", t=NT)
        Btok = take(NT * SSM_G * P).rearrange("p (t n) -> p t n", t=NT)
        W0 = at[0]
        xall = arena[:, 0:NT * D].rearrange("p (t n) -> p t n", t=NT)
        hT = take(KD * TA).rearrange("p (k t) -> p k t", k=KD)
        ABLK = 4096
        aring = [arena[:, 11000 + i * ABLK:11000 + (i + 1) * ABLK].rearrange("p (k n) -> p k n", k=KD)
                 for i in range(3)]
        lring = [arena[:, o:o + ABLK].rearrange("p (k n) -> p k n", k=KD) for o in (DN_H * TA, XT0)]
        NW = 4
        wring_all = take(NW * KD * P)
        wring = [wring_all[:, i * KD * P:(i + 1) * KD * P].rearrange("p (k n) -> p k n", k=KD) for i in range(NW)]
        wz = wring_all[:, 0:KD * 512].rearrange("p (k n) -> p k n", k=KD)
        GP = (GR + 2) * (GW + 2)
        cin_l = [take(GP).rearrange("p (r c) -> p r c", c=GW + 2) for _ in range(2)]
        cin_c = [take(TC + 2) for _ in range(2)]
        mrow = arena[0:2, at[0]:at[0] + 2 * D]
        cacc = [take(TA) for _ in range(2)]
        ctmp = take(TA)
        zst = [cacc[i][:, 0:512] for i in range(2)]

        ps = [es.enter_context(nc.psum_tensor(f"ps{i}", [P, 512], F32)) for i in range(8)]

        x_t = x.rearrange("a (t p) d -> (a t) p d", p=P)
        ctx_t = ctx.rearrange("a (t p) d -> (a t) p d", p=P)
        ada_k = ada_w.rearrange("a (k p) n -> (a p) k n", p=P)
        w_k = w_in.rearrange("a (k p) n -> (a p) k n", p=P)
        rw_k = router_w.rearrange("a (k p) n -> (a p) k n", p=P)
        taps_k = conv_w.rearrange("a (m p) i j -> (a p) m (i j)", p=P)
        NAB = 2 * D // 512
        NLB = 4 * D // 512
        LATE = 4

        tiles = []
        for i in range(DN_H):
            tiles.append((OFF_K + i * P, "k", i, True))
        for i in range(SSM_G):
            tiles.append((OFF_B + i * P, "B", i, True))
        for i in range(QK // P):
            tiles.append((OFF_V + i * P, "v", i, True))
        for i in range(DI // P):
            tiles.append((OFF_X + i * P, "x", i, True))
        for i in range(DN_H):
            tiles.append((OFF_Q + i * P, "q", i, False))
        for i in range(SSM_G):
            tiles.append((OFF_C + i * P, "C", i, False))
        NM = len(tiles)

        hflat = arena[:, W0:W0 + NT * D]
        beta_f = beta[:].rearrange("p t d h -> p t (d h)")
        eps_d, eps1, eps_q = sb("eps_d", [P, 1]), sb("eps1", [P, 1]), sb("eps_q", [P, 1])

        def n_aux(m):
            return late_before(m + 1) + sum((3 if tl[3] else 2) if tl[1] in "kq" else 3 if tl[1] in "vxB" else 0
                                            for tl in tiles[:m])

        def late_before(m):
            return min(max(m - LATE, 0), NLB)


        at[0] = W0
        L4 = DN_H * P
        kTs, kgT, qgT, E, AT, X, Y, T1, ktail, S = ([take(L4).rearrange("p (h n) -> p h n", h=DN_H)
                                                     for _ in range(2)] for _ in range(10))
        E8 = [take(SSM_H * P).rearrange("p (h n) -> p h n", h=SSM_H) for _ in range(2)]
        xdt, xw, hs = ([take(DI).rearrange("p (h n) -> p h n", h=SSM_H) for _ in range(2)] for _ in range(3))
        BTs, CTs, Bts = ([take(SSM_G * P).rearrange("p (g n) -> p g n", g=SSM_G) for _ in range(2)] for _ in range(3))
        ost = [take(QK + DI) for _ in range(2)]
        pack = take(NT * 2 * 5 * GD).rearrange("p (t d q g) -> p t d q g", t=NT, d=2, q=5)
        gs = [take(5 * GD).rearrange("p (q g) -> p q g", q=5) for _ in range(2)]
        Q_G, Q_EG, Q_EGT, Q_WT, Q_W = range(5)
        bank = [{"A": ps[4 * d], "B": ps[4 * d + 1], "C": ps[4 * d + 2], "D": ps[4 * d + 3]} for d in range(2)]
        DN, SM = slice(0, DN_H), slice(DN_H, GD)
        LV = 7

        def heads(ap, h=DN_H):
            return ap.rearrange("p (h n) -> p h n", h=h)

        def flat(ap):
            return ap.rearrange("p h n -> p (h n)")

        def bc(ap, n):
            return ap.unsqueeze(2).to_broadcast([P, ap.shape[1], n])

        def bh(ap, h=DN_H):
            return ap.unsqueeze(1).to_broadcast([P, h, ap.shape[1]])

        def tile_of(lat, t, d):
            n = NL if lat else NC
            return t + (0 if lat else NL) if d == 0 else t * -1 + (n - 1 + (0 if lat else NL))

        def count(lat, t, per_ctx, per_lat):
            return t * per_lat + NC * per_ctx if lat else per_ctx * t

        def steps(eng, body):
            for t in range(NC):
                body(False, t)
            with eng.Fori(0, NL) as t:
                body(True, t)

        D_LAT = {"sqk": 0, "g8a": 1, "g8b": 2, "sc": 3, "yoff": 4, "ydiag": 5, "st": 6, "kv": 7}
        D_CTX = {"st": 0, "kv": 1}

        def d_before(lat, t, use):
            return count(lat, t, len(D_CTX), len(D_LAT)) + (D_LAT if lat else D_CTX)[use]

        def nth(d, n):
            return n * 2 + (d - 1)

        def values(lat, t):
            def now(d, per_ctx=1, per_lat=None, i=0):
                return nth(d, count(lat, t, per_ctx, per_ctx if per_lat is None else per_lat) + i + 1)

            def past(d, per_ctx=1, per_lat=None):
                return nth(d, count(lat, t, per_ctx, per_ctx if per_lat is None else per_lat))
            return now, past

        def pe_scan(pe):
            mm, tr = nc.tensor.matmul, nc.tensor.transpose

            def rows(out, g):
                for h in range(g.shape[1]):
                    last = tr(out[:, h * P:(h + 1) * P], g[:, h:h + 1].to_broadcast([P, P]), ident[:])
                return last

            def per_head(out, lhsT, rhs):
                for h in range(DN_H):
                    last = mm(out[:, h * P:(h + 1) * P], lhsT[:, h, :], rhs[:, h, :], start=True, stop=True)
                return last

            def step(lat, t):
                now, past = values(lat, t)

                def bank_d(d, use):
                    if lat or t > 0 or D_CTX[use] > 0:
                        pe.wait_ge(sem("scan_dread"), nth(d, d_before(lat, t, use)))
                    return bank[d]["D"]

                def g8(d, half):
                    D = bank_d(d, ("g8a", "g8b")[half])
                    rows(D, gs[d][:, Q_G, DN_H + 4 * half:DN_H + 4 * half + 4]).then_inc(sem("scan_dps"), 1)

                for d in range(2):
                    pe.wait_ge(sem("scan_gs"), now(d))
                    if lat or t > 0:
                        pe.wait_ge(sem("scan_yfin"), past(d))
                    if lat:
                        pe.wait_ge(sem("scan_oc"), nth(d, t + 1))
                    rows(bank[d]["A"], gs[d][:, Q_G, DN]).then_inc(sem("scan_grow"), 1)
                for d in range(2):
                    pe.wait_ge(sem("scan_kst"), now(d))
                    if lat or t > 0:
                        pe.wait_ge(sem("scan_vnc"), past(d))
                    per_head(bank[d]["B"], kTs[d], kTs[d]).then_inc(sem("scan_skk"), 1)
                    if lat or t > 0:
                        pe.wait_ge(sem("scan_r"), past(d))
                    for h in range(DN_H):
                        last = tr(bank[d]["C"][:, h * P:(h + 1) * P], kTs[d][:, h, :], ident[:])
                    last.then_inc(sem("scan_ktr"), 1)
                    if lat:
                        D = bank_d(d, "sqk")
                        ti = tile_of(lat, t, d)
                        for h in range(DN_H):
                            last = mm(D[:, h * P:(h + 1) * P], kTs[d][:, h, :],
                                      qT[:, h, bass.ds(ti * P, P)], start=True, stop=True)
                        last.then_inc(sem("scan_dps"), 1)
                for d in range(2):
                    pe.wait_ge(sem("scan_y0"), now(d))
                    pe.wait_ge(sem("scan_egrow"), now(d))
                    pe.wait_ge(sem("scan_diff"), now(d))
                    for h in range(DN_H):
                        last = tr(bank[d]["A"][:, h * P:(h + 1) * P], Y[d][:, h, :], ident[:])
                    last.then_inc(sem("scan_xps"), 1)
                    if lat:
                        g8(d, 0)
                for lv in range(1, LV):
                    for d in range(2):
                        if lv == 1:
                            pe.wait_ge(sem("scan_x"), now(d))
                        else:
                            pe.wait_ge(sem("scan_xn"), now(d, LV - 2, i=lv - 2))
                        per_head(bank[d]["B"], AT[d], X[d]).then_inc(sem("scan_t1"), 1)
                    for d in range(2):
                        pe.wait_ge(sem("scan_t1m"), now(d, LV - 1, i=lv - 1))
                        if lv > 1:
                            pe.wait_ge(sem("scan_y"), now(d, LV - 2, i=lv - 2))
                        l, r = (Y, T1) if lv < LV - 1 else (T1, Y)
                        per_head(bank[d]["A"], l[d], r[d]).then_inc(sem("scan_xcx"), 1)
                    for d in range(2):
                        if lv < LV - 1:
                            pe.wait_ge(sem("scan_xn"), now(d, LV - 2, i=lv - 1))
                            if lv == 1:
                                pe.wait_ge(sem("scan_ktail"), now(d))
                            for h in range(DN_H):
                                last = tr(bank[d]["C"][:, h * P:(h + 1) * P], X[d][:, h, :], ident[:])
                            last.then_inc(sem("scan_yps"), 1)
                    for d in range(2):
                        if lat and lv == 1:
                            g8(d, 1)
                        if lat and lv == 2:
                            D = bank_d(d, "sc")
                            pe.wait_ge(sem("scan_cst"), now(d))
                            for g in range(SSM_G):
                                last = mm(D[:, g * P:(g + 1) * P], BTs[d][:, g, :], CTs[d][:, g, :],
                                          start=True, stop=True)
                            last.then_inc(sem("scan_dps"), 1)
                        if lat and lv == 3:
                            D = bank_d(d, "yoff")
                            for g in range(SSM_G):
                                last = mm(D[:, g * 256:(g + 1) * 256], CTs[d][:, g, :],
                                          flat(hs[d][:, g * HPG:(g + 1) * HPG, :]), start=True, stop=True)
                            last.then_inc(sem("scan_dps"), 1)
                        if lat and lv == 4:
                            D = bank_d(d, "ydiag")
                            pe.wait_ge(sem("scan_xst"), now(d))
                            for h in range(SSM_H):
                                last = mm(D[:, h * SSM_P:(h + 1) * SSM_P], E8[d][:, h, :], xdt[d][:, h, :],
                                          start=True, stop=True)
                            last.then_inc(sem("scan_dps"), 1)
                        if lv == 5:
                            D = bank_d(d, "st")
                            pe.wait_ge(sem("scan_xst"), now(d))
                            pe.wait_ge(sem("scan_cst"), now(d))
                            for g in range(SSM_G):
                                last = mm(D[:, g * 256:(g + 1) * 256], Bts[d][:, g, :],
                                          flat(xw[d][:, g * HPG:(g + 1) * HPG, :]), start=True, stop=True)
                            last.then_inc(sem("scan_dps"), 1)
                for d in range(2):
                    pe.wait_ge(sem("scan_y"), now(d, LV - 2, i=LV - 3))
                    pe.wait_ge(sem("scan_kg"), now(d))
                    if not lat and t == 0:
                        pe.wait_ge(sem("state0"), 4)
                    per_head(bank[d]["C"], kgT[d], S[d]).then_inc(sem("scan_ks"), 1)
                for d in range(2):
                    pe.wait_ge(sem("scan_r"), now(d))
                    pe.wait_ge(sem("scan_yfin"), now(d))
                    per_head(bank[d]["B"], Y[d], T1[d]).then_inc(sem("scan_vn"), 1)
                for d in range(2):
                    pe.wait_ge(sem("scan_vnc"), now(d))
                    if lat:
                        pe.wait_ge(sem("scan_qg"), now(d, 0, 1))
                        for h in range(DN_H):
                            o = bank[d]["A"][:, h * P:(h + 1) * P]
                            mm(o, qgT[d][:, h, :], S[d][:, h, :], start=True, stop=False)
                            last = mm(o, E[d][:, h, :], X[d][:, h, :], start=False, stop=True)
                        last.then_inc(sem("scan_o"), 1)
                    per_head(bank_d(d, "kv"), ktail[d], X[d]).then_inc(sem("scan_dps"), 1)

            steps(pe, step)

        def act_scan(act):
            a = nc.scalar.activation
            for i in range(2):
                act.wait_ge(sem(f"z_out{i}"), 16 * NL)
            for d in range(2):
                act.sem_inc(sem("scan_oc"), 1)

            def step(lat, t):
                now, past = values(lat, t)
                for d in range(2):
                    act.wait_ge(sem("scan_diff"), now(d))
                    a(flat(E[d]), flat(E[d]), ACT.Exp).then_inc(sem("scan_eexp"), 1)
                    if lat or t > 0:
                        act.wait_ge(sem("scan_ks"), past(d))
                    a(flat(kgT[d]), bank[d]["A"][:], ACT.Exp).then_inc(sem("scan_egrow"), 1)
                for d in range(2):
                    act.wait_ge(sem("scan_xps"), now(d))
                    a(flat(X[d]), bank[d]["A"][:], ACT.Copy).then_inc(sem("scan_x"), 1)
                for lv in range(1, LV - 1):
                    for d in range(2):
                        act.wait_ge(sem("scan_yps"), now(d, LV - 2, i=lv - 1))
                        a(flat(Y[d]), bank[d]["C"][:], ACT.Copy).then_inc(sem("scan_y"), 1)
                    if lat and lv == 1:
                        for d in range(2):
                            act.wait_ge(sem("scan_dread"), nth(d, d_before(lat, t, "g8b") + 1))
                            a(flat(E8[d]), flat(E8[d]), ACT.Exp).then_inc(sem("scan_e8"), 1)
                for d in range(2):
                    act.wait_ge(sem("scan_vn"), now(d))
                    a(flat(X[d]), bank[d]["B"][:], ACT.Copy).then_inc(sem("scan_vnc"), 1)
                if lat:
                    for d in range(2):
                        act.wait_ge(sem("scan_o"), now(d, 0, 1))
                        act.wait_ge(sem(f"ost_out{d}"), t * 16 + 16)
                        a(ost[d][:, 0:QK], bank[d]["A"][:], ACT.Copy).then_inc(sem("scan_oc"), 1)

            steps(act, step)

        def dve_scan(dve, link):
            v = nc.vector

            def pk(q, g0, src, n):
                for d in range(2):
                    ins = v.tensor_copy(pack[:, :, d, q, g0:g0 + n], src[:, :, d, :])
                return ins

            dve.wait_ge(sem("zps"), 2 * NL)
            for i in range(2):
                dve.wait_ge(sem(f"z_out{i}"), 16 * NL)
            pk(Q_G, 0, G, GD)
            pk(Q_EG, 0, eG, GD)
            pk(Q_EGT, 0, eGt, GD)
            dve.wait_ge(sem("wtail"), 2)
            pk(Q_WT, 0, wtail, GD)
            pk(Q_W, 0, beta, DN_H)
            pk(Q_W, DN_H, sp[:, :, :, SM], SSM_H).then_inc(sem("pack"), 1)
            for d in range(2):
                v.memset(S[d], 0.0).then_inc(sem("state0"), 1)
                v.memset(hs[d], 0.0).then_inc(sem("state0"), 1)

            def step(lat, t):
                now, past = values(lat, t)

                def d_full(d, use):
                    dve.wait_ge(sem("scan_dps"), nth(d, d_before(lat, t, use) + 1))
                    return bank[d]["D"]

                def diff(d, out, src, g0):
                    for h in range(4):
                        ins = v.scalar_tensor_tensor(out[:, h, :], src[:, h * P:(h + 1) * P],
                                                     gs[d][:, Q_G, g0 + h:g0 + h + 1], neg_mask[:, d, :],
                                                     ALU.subtract, ALU.min)
                    return ins

                def g8(d, half):
                    D = d_full(d, ("g8a", "g8b")[half])
                    diff(d, E8[d][:, 4 * half:4 * half + 4, :], D, DN_H + 4 * half).then_inc(sem("scan_dread"), 1)

                for d in range(2):
                    dve.wait_ge(sem("scan_grow"), now(d))
                    if lat:
                        dve.wait_ge(sem("scan_oc"), nth(d, t + 1))
                    diff(d, E[d], bank[d]["A"], 0).then_inc(sem("scan_diff"), 1)
                for d in range(2):
                    dve.wait_ge(sem("scan_skk"), now(d))
                    dve.wait_ge(sem("scan_ebeta"), now(d))
                    v.tensor_tensor(AT[d], heads(bank[d]["B"][:]), E[d], ALU.mult).then_inc(sem("scan_at"), 1)
                    dve.wait_ge(sem("scan_ktr"), now(d))
                    v.tensor_tensor(ktail[d], heads(bank[d]["C"][:]), bc(gs[d][:, Q_WT, DN], P), ALU.mult)\
                        .then_inc(sem("scan_ktail"), 1)
                    dve.wait_ge(sem("scan_at"), now(d))
                    v.scalar_tensor_tensor(Y[d], AT[d], -1.0, bh(lvl_mask[:, 1 - d, 0, :]), ALU.mult, ALU.mult)\
                        .then_inc(sem("scan_y0a"), 1)
                    if lat:
                        D = d_full(d, "sqk")
                        v.tensor_tensor(E[d], heads(D[:]), E[d], ALU.mult).then_inc(sem("scan_dread"), 1)
                    dve.wait_ge(sem("scan_y0a"), now(d))
                    v.tensor_tensor(Y[d], Y[d], bh(ident[:]), ALU.add).then_inc(sem("scan_y0"), 1)
                if lat:
                    for d in range(2):
                        g8(d, 0)
                for lv in range(1, LV):
                    for d in range(2):
                        dve.wait_ge(sem("scan_t1"), now(d, LV - 1, i=lv - 1))
                        v.tensor_tensor(T1[d], heads(bank[d]["B"][:]), bh(lvl_mask[:, d, lv, :]), ALU.mult)\
                            .then_inc(sem("scan_t1m"), 1)
                    for d in range(2):
                        dve.wait_ge(sem("scan_xcx"), now(d, LV - 1, i=lv - 1))
                        if lv < LV - 1:
                            if lv > 1:
                                dve.wait_ge(sem("scan_xn"), now(d, LV - 2, i=lv - 2))
                            v.tensor_tensor(X[d], X[d], heads(bank[d]["A"][:]), ALU.subtract)\
                                .then_inc(sem("scan_xn"), 1)
                        else:
                            v.tensor_tensor(Y[d], Y[d], heads(bank[d]["A"][:]), ALU.subtract)\
                                .then_inc(sem("scan_yfin"), 1)
                    for d in range(2):
                        if lat and lv == 1:
                            g8(d, 1)
                        if lat and lv == 2:
                            D = d_full(d, "sc")
                            dve.wait_ge(sem("scan_e8"), now(d, 0, 1))
                            for g in range(SSM_G):
                                hh = slice(g * HPG, (g + 1) * HPG)
                                ins = v.tensor_tensor(E8[d][:, hh, :], E8[d][:, hh, :],
                                                      bh(D[:, g * P:(g + 1) * P], HPG), ALU.mult)
                            ins.then_inc(sem("scan_dread"), 1)
                        if lat and lv == 3:
                            D = d_full(d, "yoff")
                            dve.wait_ge(sem(f"ost_out{d}"), t * 16 + 16)
                            v.tensor_tensor(heads(ost[d][:, QK:QK + DI], SSM_H), heads(D[:], SSM_H),
                                            bc(gs[d][:, Q_EG, SM], SSM_P), ALU.mult).then_inc(sem("scan_dread"), 1)
                        if lat and lv == 4:
                            D = d_full(d, "ydiag")
                            dve.wait_ge(sem("scan_dread"), nth(d, d_before(lat, t, "yoff") + 1))
                            v.tensor_tensor(ost[d][:, QK:QK + DI], ost[d][:, QK:QK + DI], D[:], ALU.add)\
                                .then_inc(sem("scan_dread"), 1)
                        if lv == 5:
                            D = d_full(d, "st")
                            dve.wait_ge(sem("scan_hg"), now(d))
                            v.tensor_tensor(hs[d], hs[d], heads(D[:], SSM_H), ALU.add).then_inc(sem("scan_dread"), 1)
                for d in range(2):
                    dve.wait_ge(sem("scan_ks"), now(d))
                    ti = tile_of(lat, t, d)
                    v.tensor_tensor(flat(T1[d]), vtok[:, bass.ds(ti, 1), :].rearrange("p a n -> p (a n)"),
                                    bank[d]["C"][:], ALU.subtract).then_inc(sem("scan_r"), 1)
                for d in range(2):
                    D = d_full(d, "kv")
                    dve.wait_ge(sem("scan_sg"), now(d))
                    v.tensor_tensor(S[d], S[d], heads(D[:]), ALU.add).then_inc(sem("scan_dread"), 1)

            steps(dve, step)

        def pool_scan(pool):
            p = nc.gpsimd

            def step(lat, t):
                now, past = values(lat, t)
                ti = [tile_of(lat, t, d) for d in range(2)]

                def done(d):
                    if lat or t > 0:
                        pool.wait_ge(sem("scan_dread"), past(d, len(D_CTX), len(D_LAT)))

                for d in range(2):
                    done(d)
                    p.tensor_copy(gs[d].rearrange("p q g -> p (q g)"),
                                  pack[:, bass.ds(ti[d], 1), d, :, :].rearrange("p a q g -> p (a q g)"))\
                        .then_inc(sem("scan_gs"), 1)
                    p.tensor_copy(kTs[d], kT[:, :, bass.ds(ti[d] * P, P)]).then_inc(sem("scan_kst"), 1)
                for d in range(2):
                    if lat:
                        p.tensor_copy(BTs[d], BT[:, :, bass.ds(ti[d] * P, P)])
                        p.tensor_copy(CTs[d], CT[:, :, bass.ds(ti[d] * P, P)])
                    p.tensor_copy(flat(Bts[d]), Btok[:, bass.ds(ti[d], 1), :].rearrange("p a n -> p (a n)"))\
                        .then_inc(sem("scan_cst"), 1)
                for d in range(2):
                    pool.wait_ge(sem("scan_gs"), now(d))
                    pool.wait_ge(sem("scan_eexp"), now(d))
                    p.tensor_tensor(E[d], E[d], bc(gs[d][:, Q_W, DN], P), ALU.mult).then_inc(sem("scan_ebeta"), 1)
                for d in range(2):
                    xt = xtok[:, bass.ds(ti[d], 1), :].rearrange("p a (h n) -> p (a h) n", h=SSM_H)
                    p.tensor_tensor(xdt[d], xt, bc(gs[d][:, Q_W, SM], SSM_P), ALU.mult)
                    p.tensor_tensor(xw[d], xt, bc(gs[d][:, Q_WT, SM], SSM_P), ALU.mult).then_inc(sem("scan_xst"), 1)
                for d in range(2):
                    pool.wait_ge(sem("scan_egrow"), now(d))
                    if lat:
                        p.tensor_tensor(qgT[d], qT[:, :, bass.ds(ti[d] * P, P)], kgT[d], ALU.mult)\
                            .then_inc(sem("scan_qg"), 1)
                    pool.wait_ge(sem("scan_kst"), now(d))
                    p.tensor_tensor(kgT[d], kTs[d], kgT[d], ALU.mult).then_inc(sem("scan_kg"), 1)
                for d in range(2):
                    if lat:
                        pool.wait_ge(sem("scan_dps"), nth(d, d_before(lat, t, "yoff") + 1))
                    elif t == 0 and d == 0:
                        pool.wait_ge(sem("state0"), 4)
                    p.tensor_tensor(hs[d], hs[d], bc(gs[d][:, Q_EGT, SM], SSM_P), ALU.mult).then_inc(sem("scan_hg"), 1)
                for d in range(2):
                    pool.wait_ge(sem("scan_ks"), now(d))
                    if lat:
                        pool.wait_ge(sem("scan_o"), now(d, 0, 1))
                    p.tensor_tensor(S[d], S[d], bc(gs[d][:, Q_EGT, DN], P), ALU.mult).then_inc(sem("scan_sg"), 1)

            pool.wait_ge(sem("pack"), 1)
            steps(pool, step)

        def sp_scan(sp_):
            for d in range(2):
                sp_.sem_inc(sem(f"ost_out{d}"), 16)
            with sp_.Fori(0, NL) as t:
                for d in range(2):
                    sp_.wait_ge(sem("scan_oc"), nth(d, t + 2))
                    sp_.wait_ge(sem("scan_dread"), nth(d, d_before(True, t, "ydiag") + 1))
                    sp_.dma_start(scan_dram[d, bass.ds(tile_of(True, t, d), 1), :, :].rearrange("a p n -> (a p) n"),
                                  ost[d]).then_inc(sem(f"ost_out{d}"), 16)
            for d in range(2):
                sp_.wait_ge(sem(f"ost_out{d}"), 16 * (NL + 1))

        at[0] = 0
        fb = [take(D) for _ in range(2)]
        bb = [take(D) for _ in range(2)]
        zb_ = [take(D) for _ in range(2)]
        xr = [take(D) for _ in range(2)]
        mixT = [take(D).rearrange("p (k n) -> p k n", k=KD) for _ in range(2)]
        h2 = [take(D) for _ in range(2)]
        h2T = [take(D).rearrange("p (k n) -> p k n", k=KD) for _ in range(2)]
        rowv = take(3 * D).rearrange("p (r n) -> p r n", r=3)
        zero = take(D // 2)
        assert at[0] <= XT0
        at[0] = W0
        wo = take(KD * D).rearrange("p (k n) -> p k n", k=KD)
        x2 = take(NL * D).rearrange("p (t n) -> p t n", t=NL)
        affT = take(T)[0:E_N, :]
        row5 = take(D)
        aff = take(NL * E_N).rearrange("p (t n) -> p t n", t=NL)
        sqj = take(D)
        tk = take(3 * P)
        topv, topf = tk[0:E_N, 0:CAP], tk[0:E_N, CAP:2 * CAP]
        topi = take(P).bitcast(U32)[0:E_N, 0:CAP]
        idxT = take(E_N).bitcast(U32)
        gateT = take(E_N)
        rcol = take(4 * KD).rearrange("p (r k) -> p r k", r=4)
        sq, rs, sm = ([take(8) for _ in range(2)] for _ in range(3))
        lmax = take(NL)
        at[0] = 0
        ew = []
        for _ in range(2):
            wg = take(KD * F).rearrange("p (k n) -> p k n", k=KD)
            wu = take(KD * F).rearrange("p (k n) -> p k n", k=KD)
            wd = take(KF * D).rearrange("p (k n) -> p k n", k=KF)
            ew.append((wg, wu, wd))
        NX = 4
        xs = [take(D) for _ in range(NX)]
        xsT = [take(D).rearrange("p (k n) -> p k n", k=KD) for _ in range(2)]
        hid = [take(F) for _ in range(2)]
        hidT = [take(F).rearrange("p (k n) -> p k n", k=KF) for _ in range(2)]
        ye = [take(D) for _ in range(2)]
        assert at[0] <= W0 + KD * D
        yt = arena[:, 0:NL * D].rearrange("p (t n) -> p t n", t=NL)

        wo_k = w_out.rearrange("a (k p) n -> (a p) k n", p=P)
        wg_e = exp_w_gate.rearrange("a e (k p) n -> (a e) p k n", p=P)
        wu_e = exp_w_up.rearrange("a e (k p) n -> (a e) p k n", p=P)
        wd_e = exp_w_down.rearrange("a e (k p) n -> (a e) p k n", p=P)
        h2_t = h2_dram.rearrange("(t p) d -> t p d", p=P)
        y_t = y_dram.rearrange("(t p) d -> t p d", p=P)
        out_t = out.rearrange("a (t p) d -> (a t) p d", p=P)
        N_SCAN = count(True, NL, len(D_CTX), len(D_LAT))

        def scan_over(eng):
            for d in range(2):
                eng.wait_ge(sem("scan_dread"), nth(d, N_SCAN))
                eng.wait_ge(sem("scan_oc"), nth(d, NL + 1))
                eng.wait_ge(sem(f"ost_out{d}"), 16 * (NL + 1))

        def sp_tail(sp_):
            scan_over(sp_)

            def load(t):
                s = t % 2
                if t >= 2:
                    sp_.wait_ge(sem("fbT"), t - 1)
                for dst, src in ((fb[s], scan_dram[0, t]), (bb[s], scan_dram[1, t]), (zb_[s], z_dram[t])):
                    sp_.dma_start(dst, src).then_inc(sem(f"m_in{s}"), 16)
                if t >= 2:
                    sp_.wait_ge(sem("x2"), t - 1)
                sp_.dma_start(xr[s], x_t[t]).then_inc(sem(f"xr_in{s}"), 16)
            load(0)
            for k in range(0, KD, 2):
                sp_.dma_start(wo[:, k:k + 2, :], wo_k[:, k:k + 2, :]).then_inc(sem("wo_in"), 16)
            load(1)
            sp_.wait_ge(sem("zero"), 1)
            for t in range(NL):
                for h in range(2):
                    sp_.dma_start(y_t[t, :, h * 512:(h + 1) * 512], zero).then_inc(sem("y_zero"), 16)
            for t in range(NL):
                if t + 2 < NL:
                    load(t + 2)
                sp_.wait_ge(sem("h2"), t + 1)
                sp_.dma_start(h2_t[t], h2[t % 2]).then_inc(sem(f"h2_out{t % 2}"), 16)
            sp_.wait_ge(sem("h2ps"), NL)
            sp_.wait_ge(sem("mps"), NL)
            for i in range(2):
                sp_.wait_ge(sem(f"h2_out{i}"), 16 * NL // 2)

            def load_expert(e, s):
                sp_.dma_start(ew[s][0], wg_e[e]).then_inc(sem(f"gu_in{s}"), 16)
                sp_.dma_start(ew[s][1], wu_e[e]).then_inc(sem(f"gu_in{s}"), 16)
                sp_.dma_start(ew[s][2], wd_e[e]).then_inc(sem(f"d_in{s}"), 16)
            for e in range(E_N):
                if e == 1:
                    sp_.wait_ge(sem("logit"), NL)
                    sp_.wait_ge(sem("y_zero"), 32 * NL)
                if e >= 2:
                    sp_.wait_ge(sem("down"), e - 1)
                load_expert(e, e % 2)
            sp_.wait_ge(sem("y_sc"), 16 * E_N)
            sp_.wait_ge(sem("down"), E_N)
            for t in range(NL):
                sp_.dma_start(yt[:, t, :], y_t[t]).then_inc(sem(f"tile_in{t // 2}"), 16)
            for t in range(NL):
                sp_.wait_ge(sem("fin"), t + 1)
                sp_.dma_start(out_t[t], yt[:, t, :]).then_inc(sem("out"), 16)
            sp_.wait_ge(sem("out"), 16 * NL)

        def pe_tail(pe):
            mm, tr = nc.tensor.matmul, nc.tensor.transpose
            scan_over(pe)
            for r in range(4):
                if r >= 1:
                    pe.wait_ge(sem("rowv"), r)
                else:
                    pe.wait_ge(sem("rcol"), 1)
                for k in range(KD):
                    last = tr(ps[k // 4][:, (k % 4) * P:(k % 4 + 1) * P], rcol[:, r, k:k + 1].to_broadcast([P, P]),
                              ident[:])
                last.then_inc(sem("rowps"), 1)
            pe.wait_ge(sem("rowv"), 4)

            def back(t):
                s = t % 2
                pe.wait_ge(sem("h2"), t + 1)
                if t >= 1:
                    pe.wait_ge(sem("h2T"), t)
                for k in range(KD):
                    last = tr(ps[6 + k // 4][:, (k % 4) * P:(k % 4 + 1) * P], h2[s][:, k * P:(k + 1) * P], ident[:])
                last.then_inc(sem("h2ps"), 1)

            def router(t):
                s = t % 2
                pe.wait_ge(sem("h2T"), t + 1)
                if t >= 1:
                    pe.wait_ge(sem("lcopy"), t)
                for k in range(KD):
                    last = mm(ps[1][:, 0:E_N], h2T[s][:, k, :], rw[:, k, :], start=(k == 0), stop=(k == KD - 1))
                last.then_inc(sem("logit"), 1)

            for t in range(NL):
                s = t % 2
                pe.wait_ge(sem("mixed"), t + 1)
                if t >= 3:
                    pe.wait_ge(sem("lcopy"), t - 2)
                for k in range(KD):
                    last = tr(ps[k // 4][:, (k % 4) * P:(k % 4 + 1) * P], fb[s][:, k * P:(k + 1) * P], ident[:])
                last.then_inc(sem("fbT"), 1)
                if t >= 2:
                    back(t - 2)
                pe.wait_ge(sem("mixT"), t + 1)
                if t == 0:
                    pe.wait_ge(sem("wo_in"), 16 * KD // 2)
                if t >= 2:
                    pe.wait_ge(sem("x2"), t - 1)
                for h in range(2):
                    for k in range(KD):
                        last = mm(ps[2 + 2 * s + h][:], mixT[s][:, k, :], wo[:, k, h * 512:(h + 1) * 512],
                                  start=(k == 0), stop=(k == KD - 1))
                    if h == 0 and t >= 2:
                        router(t - 2)
                last.then_inc(sem("mps"), 1)
            for t in range(NL - 2, NL):
                back(t)
                router(t)
            pe.wait_ge(sem("aff"), 1)
            for t in range(NL):
                last = tr(ps[2 + t // 4][0:E_N, (t % 4) * P:(t % 4 + 1) * P], aff[:, t, :], ident[:])
            last.then_inc(sem("affps"), 1)
            pe.wait_ge(sem("topk"), 2)
            tr(ps[0][:, 0:E_N], topf, ident[0:E_N, 0:E_N])
            tr(ps[0][:, E_N:2 * E_N], topv, ident[0:E_N, 0:E_N]).then_inc(sem("topT"), 1)
            pe.wait_ge(sem("idx"), 2)

            def xs_transposed(e):
                pe.wait_ge(sem(f"xs_in{e % NX}"), 16 * (e // NX + 1))
                if e >= 1:
                    pe.wait_ge(sem("xsT"), e)
                for k in range(KD):
                    last = tr(ps[k // 4][:, (k % 4) * P:(k % 4 + 1) * P], xs[e % NX][:, k * P:(k + 1) * P], ident[:])
                last.then_inc(sem("xsps"), 1)

            xs_transposed(0)
            for e in range(E_N):
                s = e % 2
                pe.wait_ge(sem("xsT"), e + 1)
                pe.wait_ge(sem(f"gu_in{s}"), 32 * (e // 2 + 1))
                if e >= 1:
                    pe.wait_ge(sem("hidT"), e)
                for j in range(2):
                    for k in range(KD):
                        last = mm(ps[2 + j][:], xsT[s][:, k, :], ew[s][j][:, k, :], start=(k == 0), stop=(k == KD - 1))
                last.then_inc(sem("gu"), 1)
                if e + 1 < E_N:
                    xs_transposed(e + 1)
                pe.wait_ge(sem("hid"), e + 1)
                for k in range(KF):
                    last = tr(ps[4][:, k * P:(k + 1) * P], hid[s][:, k * P:(k + 1) * P], ident[:])
                last.then_inc(sem("hidps"), 1)
                pe.wait_ge(sem("hidT"), e + 1)
                pe.wait_ge(sem(f"d_in{s}"), 16 * (e // 2 + 1))
                if e >= 1:
                    pe.wait_ge(sem("ye"), e)
                for h in range(2):
                    for k in range(KF):
                        last = mm(ps[5 + h][:], hidT[s][:, k, :], ew[s][2][:, k, h * 512:(h + 1) * 512],
                                  start=(k == 0), stop=(k == KF - 1))
                last.then_inc(sem("down"), 1)

        def act_tail(act):
            a = nc.scalar.activation
            scan_over(act)

            def sqrt_of(src, dst, n, name, c):
                a(dst, src, ACT.Sqrt, scale=1.0 / n, bias=eps1[:]).then_inc(sem(name), c)

            def front(t):
                s = t % 2
                act.wait_ge(sem("merged"), t + 1)
                if t == 0:
                    act.wait_ge(sem("rowps"), 4)
                for h in range(DN_H):
                    a(sqj[:, h * P:(h + 1) * P], fb[s][:, h * P:(h + 1) * P], ACT.Square, accum_out=sq[s][:, h:h + 1])
                for g in range(SSM_G):
                    last = a(sqj[:, QK + g * 256:QK + (g + 1) * 256], fb[s][:, QK + g * 256:QK + (g + 1) * 256],
                             ACT.Square, accum_out=sq[s][:, DN_H + g:DN_H + g + 1])
                last.then_inc(sem("fsq"), 1)
                act.wait_ge(sem("fsq"), t + 1)
                a(rs[s][:, 0:DN_H], sq[s][:, 0:DN_H], ACT.Sqrt, scale=1.0 / P, bias=eps1[:])
                sqrt_of(sq[s][:, DN_H:DN_H + SSM_G], rs[s][:, DN_H:DN_H + SSM_G], DI // SSM_G, "fsqrt", 1)

            def mix_t(t):
                s = t % 2
                act.wait_ge(sem("fbT"), t + 1)
                if t >= 2:
                    act.wait_ge(sem("mps"), t - 1)
                a(mixT[s][:, 0:DN_H, :], heads(ps[0][:]), ACT.Copy, scale=vcols[:, V_DG:V_DG + 1])
                for k in range(4):
                    last = a(mixT[s][:, 4 + k, :], ps[1][:, k * P:(k + 1) * P], ACT.Copy,
                             scale=vcols[:, V_SG + k:V_SG + k + 1])
                last.then_inc(sem("mixT"), 1)

            def back_sum(t):
                s = t % 2
                act.wait_ge(sem("mps"), t + 1)
                if t >= 1:
                    act.wait_ge(sem("bsq"), 4 * t)
                for h in range(2):
                    a(sqj[:, h * 512:(h + 1) * 512], ps[2 + 2 * s + h][:], ACT.Square, accum_out=sm[s][:, h:h + 1])\
                        .then_inc(sem("bsq"), 1)
                act.wait_ge(sem("msum"), t + 1)
                a(sm[s][:, 2:3], sm[s][:, 2:3], ACT.Sqrt, scale=1.0 / D, bias=eps1[:]).then_inc(sem("bsqrt"), 1)

            def back_x2(t):
                s = t % 2
                act.wait_ge(sem("x2"), t + 1)
                a(sqj[:, 0:D], x2[:, t, :], ACT.Square, accum_out=sm[s][:, 3:4]).then_inc(sem("bsq"), 1)
                act.wait_ge(sem("bsq"), 4 * t + 3)
                a(sm[s][:, 3:4], sm[s][:, 3:4], ACT.Sqrt, scale=1.0 / D, bias=eps1[:]).then_inc(sem("bsq"), 1)

            def h2_t(t):
                s = t % 2
                act.wait_ge(sem("h2ps"), t + 1)
                if t >= 2:
                    act.wait_ge(sem("logit"), t - 1)
                for h in range(2):
                    last = a(h2T[s][:, 4 * h:4 * h + 4, :], heads(ps[6 + h][:]), ACT.Copy)
                last.then_inc(sem("h2T"), 1)

            front(0)
            for t in range(NL + 2):
                if t + 1 < NL:
                    front(t + 1)
                if t < NL:
                    mix_t(t)
                if t >= 2:
                    h2_t(t - 2)
                if 1 <= t <= NL:
                    back_sum(t - 1)
                    back_x2(t - 1)
            act.wait_ge(sem("lmax"), 1)
            a(aff, aff, ACT.Exp).then_inc(sem("lexp"), 1)
            act.wait_ge(sem("affps"), 1)
            for h in range(2):
                a(affT[:, h * 512:(h + 1) * 512], ps[2 + h][0:E_N, :], ACT.Copy).then_inc(sem("affT"), 1)
            for e in range(E_N + 1):
                if e < E_N:
                    s = e % 2
                    act.wait_ge(sem("xsps"), e + 1)
                    if e >= 2:
                        act.wait_ge(sem("gu"), e - 1)
                    for h in range(2):
                        last = a(xsT[s][:, 4 * h:4 * h + 4, :], heads(ps[h][:]), ACT.Copy)
                    last.then_inc(sem("xsT"), 1)
                if e >= 1:
                    s = (e - 1) % 2
                    act.wait_ge(sem("hidps"), e)
                    a(hidT[s], heads(ps[4][:]), ACT.Copy).then_inc(sem("hidT"), 1)
                if e < E_N:
                    s = e % 2
                    act.wait_ge(sem("gu"), e + 1)
                    a(hid[s], ps[2][:], ACT.Silu).then_inc(sem("sg"), 1)
            for t in range(NL):
                act.wait_ge(sem(f"tile_in{t // 2}"), 64)
                a(x2dead, yt[:, t, :], ACT.Square, accum_out=ssq[:, t:t + 1]).then_inc(sem("ysq"), 1)
                act.wait_ge(sem("ysq"), 2 * t + 1)
                a(rstd[:, t:t + 1], ssq[:, t:t + 1], ACT.Sqrt, scale=1.0 / D, bias=eps1[:]).then_inc(sem("ysq"), 1)
        x2dead = sqj

        def dve_tail(dve, link):
            v = nc.vector
            scan_over(dve)
            m = mods[:, :, 0]
            g = vcols[:, V_NG:V_CB].rearrange("p (r k) -> p r k", k=KD)
            link(v.tensor_tensor(m[:, 2 * KD:6 * KD], m[:, 2 * KD:6 * KD], vcols[:, V_AB + 2 * KD:V_NG], ALU.add))
            v.tensor_tensor(rcol[:, 0, :], m[:, 2 * KD:3 * KD], g[:, 1, :], ALU.mult)
            v.scalar_tensor_tensor(rcol[:, 1, :], m[:, 4 * KD:5 * KD], 1.0, g[:, 2, :], ALU.add, ALU.mult)
            v.tensor_copy(rcol[:, 2, :], m[:, 3 * KD:4 * KD])
            v.tensor_tensor(rcol[:, 3, :], m[:, 5 * KD:6 * KD], g[:, 3, :], ALU.mult).then_inc(sem("rcol"), 1)
            for r in range(4):
                dve.wait_ge(sem("rowps"), r + 1)
                dst = rowv[:, r, :] if r < 3 else row5
                v.tensor_copy(dst[:, 0:512], ps[0][:])
                v.tensor_copy(dst[:, 512:D], ps[1][:]).then_inc(sem("rowv"), 1)

            def front(t):
                s = t % 2
                dve.wait_ge(sem(f"m_in{s}"), 48 * (t // 2 + 1))
                link(v.tensor_tensor(fb[s], fb[s], bb[s], ALU.add))
                link(v.tensor_tensor(heads(bb[s][:, QK:D], SSM_H),
                                     xtok[:, t, :].rearrange("p (h n) -> p h n", h=SSM_H),
                                     bc(sbc[:, 48:56], SSM_P), ALU.mult))
                link(v.tensor_tensor(fb[s][:, QK:D], fb[s][:, QK:D], bb[s][:, QK:D], ALU.add))
                v.tensor_tensor(fb[s][:, QK:D], fb[s][:, QK:D], zb_[s][:, QK:D], ALU.mult).then_inc(sem("merged"), 1)

            def front_r(t):
                s = t % 2
                dve.wait_ge(sem("fsqrt"), t + 1)
                link(v.reciprocal(rs[s][:, 0:6], rs[s][:, 0:6]))
                link(v.tensor_tensor(heads(fb[s][:, 0:QK]), heads(fb[s][:, 0:QK]), bc(rs[s][:, 0:DN_H], P), ALU.mult))
                v.tensor_tensor(fb[s][:, 0:QK], fb[s][:, 0:QK], zb_[s][:, 0:QK], ALU.mult)
                v.tensor_tensor(heads(fb[s][:, QK:D], SSM_G), heads(fb[s][:, QK:D], SSM_G),
                                bc(rs[s][:, DN_H:6], 256), ALU.mult).then_inc(sem("mixed"), 1)

            def back_sum(t):
                s = t % 2
                dve.wait_ge(sem("bsq"), 4 * t + 2)
                v.tensor_tensor(sm[s][:, 2:3], sm[s][:, 0:1], sm[s][:, 1:2], ALU.add).then_inc(sem("msum"), 1)

            def back_x2(t):
                s = t % 2
                dve.wait_ge(sem("bsqrt"), t + 1)
                link(v.reciprocal(sm[s][:, 2:3], sm[s][:, 2:3]))
                for h in range(2):
                    hs_ = slice(h * 512, (h + 1) * 512)
                    ins = v.scalar_tensor_tensor(x2[:, t, hs_], ps[2 + 2 * s + h][:], sm[s][:, 2:3], rowv[:, 0, hs_],
                                                 ALU.mult, ALU.mult)
                link(ins)
                dve.wait_ge(sem(f"xr_in{s}"), 16 * (t // 2 + 1))
                v.tensor_tensor(x2[:, t, :], x2[:, t, :], xr[s], ALU.add).then_inc(sem("x2"), 1)

            def back_h2(t):
                s = t % 2
                dve.wait_ge(sem("bsq"), 4 * t + 4)
                link(v.reciprocal(sm[s][:, 3:4], sm[s][:, 3:4]))
                if t >= 2:
                    dve.wait_ge(sem(f"h2_out{s}"), 16 * (t // 2))
                    dve.wait_ge(sem("h2ps"), t - 1)
                link(v.scalar_tensor_tensor(h2[s], x2[:, t, :], sm[s][:, 3:4], rowv[:, 1, :], ALU.mult, ALU.mult))
                v.tensor_tensor(h2[s], h2[s], rowv[:, 2, :], ALU.add).then_inc(sem("h2"), 1)

            front(0)
            for t in range(NL + 2):
                if t < NL:
                    front_r(t)
                if t + 1 < NL:
                    front(t + 1)
                if 1 <= t <= NL:
                    back_sum(t - 1)
                    back_x2(t - 1)
                    back_h2(t - 1)
                if t >= 2:
                    dve.wait_ge(sem("logit"), t - 1)
                    v.tensor_copy(aff[:, t - 2, :], ps[1][:, 0:E_N]).then_inc(sem("lcopy"), 1)
            dve.wait_ge(sem("lcopy"), NL)
            link(v.reduce_max(lmax, aff, AX.X))
            v.tensor_tensor(aff, aff, bc(lmax, E_N), ALU.subtract).then_inc(sem("lmax"), 1)
            dve.wait_ge(sem("lexp"), 1)
            link(v.reduce_sum(lmax, aff, AX.X))
            link(v.reciprocal(lmax, lmax))
            v.tensor_tensor(aff, aff, bc(lmax, E_N), ALU.mult).then_inc(sem("aff"), 1)
            dve.wait_ge(sem("affT"), 2)
            for r in range(CAP // 8):
                c = slice(8 * r, 8 * r + 8)
                link(v.max(topv[:, c], affT))
                link(v.max_index(topi[:, c], topv[:, c], affT))
                if r < CAP // 8 - 1:
                    link(v.match_replace(affT, topv[:, c], affT, -1.0))
            v.tensor_copy(topf, topi).then_inc(sem("topk"), 2)
            dve.wait_ge(sem("topT"), 1)
            v.tensor_copy(idxT, ps[0][:, 0:E_N]).then_inc(sem("idx"), 1)
            v.tensor_copy(gateT, ps[0][:, E_N:2 * E_N]).then_inc(sem("idx"), 1)
            dve.wait_ge(sem("idx"), 2)
            for e in range(E_N):
                s = e % 2
                dve.wait_ge(sem("sg"), e + 1)
                v.tensor_tensor(hid[s], hid[s], ps[3][:], ALU.mult).then_inc(sem("hid"), 1)
                dve.wait_ge(sem("down"), e + 1)
                if e >= 2:
                    dve.wait_ge(sem("y_sc"), 16 * (e - 1))
                v.tensor_scalar(ye[s][:, 0:512], ps[5][:], gateT[:, e:e + 1], None, ALU.mult)
                v.tensor_scalar(ye[s][:, 512:D], ps[6][:], gateT[:, e:e + 1], None, ALU.mult).then_inc(sem("ye"), 1)
            for t in range(NL):
                dve.wait_ge(sem("ysq"), 2 * t + 2)
                link(v.reciprocal(rstd[:, t:t + 1], rstd[:, t:t + 1]))
                link(v.scalar_tensor_tensor(yt[:, t, :], yt[:, t, :], rstd[:, t:t + 1], row5, ALU.mult, ALU.mult))
                v.tensor_tensor(yt[:, t, :], yt[:, t, :], x2[:, t, :], ALU.add).then_inc(sem("fin"), 1)

        def pool_tail(pool):
            p = nc.gpsimd
            scan_over(pool)
            p.memset(zero, 0.0).then_inc(sem("zero"), 1)
            pool.wait_ge(sem("idx"), 2)
            for i in range(2):
                pool.wait_ge(sem(f"h2_out{i}"), 16 * NL // 2)
            pool.wait_ge(sem("y_zero"), 32 * NL)

            def gather(e):
                p.indirect_dma_start(xs[e % NX], None, h2_dram,
                                     bass.IndirectOffsetOnAxis(ap=idxT[:, e:e + 1], axis=0))\
                    .then_inc(sem(f"xs_in{e % NX}"), 16)
            for e in range(NX):
                gather(e)
            for e in range(E_N):
                if 1 <= e <= E_N - NX:
                    pool.wait_ge(sem("xsps"), e)
                    gather(e + NX - 1)
                pool.wait_ge(sem("ye"), e + 1)
                if e >= 1:
                    pool.wait_ge(sem("y_sc"), 16 * e)
                p.indirect_dma_start(y_dram, bass.IndirectOffsetOnAxis(ap=idxT[:, e:e + 1], axis=0), ye[e % 2], None,
                                     compute_op=ALU.add).then_inc(sem("y_sc"), 16)

        N_C1 = [5 + 2 * 7 * 3]
        block = es.enter_context(nc.Block())

        small = [(vrows[V_C:V_CC, :], c.rearrange("a (j p) -> (a j) p", p=P)),
                 (vrows[V_CC:V_AB, :], c_ctx.rearrange("(j p) -> j p", p=P)),
                 (vrows[V_AB:V_NG, :], ada_b.rearrange("a (j p) -> (a j) p", p=P)),
                 (vrows[V_NG:V_CB, :], norm_g.rearrange("a b (j p) -> (a b j) p", p=P)),
                 (vrows[V_CB:V_DG, :], conv_b.rearrange("a (j p) -> (a j) p", p=P)),
                 (vrows[V_DG:V_SG, :], dn_norm_g),
                 (vrows[V_SG:NV, :], ssm_norm_g.rearrange("a (j p) -> (a j) p", p=P)),
                 (srow[0:1, 0:24].rearrange("o (d g) -> o d g", d=2)[:, :, 0:DN_H], dn_dt_bias),
                 (srow[0:1, 0:24].rearrange("o (d g) -> o d g", d=2)[:, :, DN_H:GD], ssm_dt_bias),
                 (srow[0:1, 24:48].rearrange("o (d g) -> o d g", d=2)[:, :, 0:DN_H], dn_A_log),
                 (srow[0:1, 24:48].rearrange("o (d g) -> o d g", d=2)[:, :, DN_H:GD], ssm_A_log),
                 (srow[0:1, 48:56], ssm_D)]

        def late_load(b):
            nc.sync.dma_start(lring[b % 2], ada_k[:, :, (NAB + b) * 512:(NAB + b + 1) * 512])\
                .then_inc(sem(f"late_in{b % 2}"), 16)

        @block.sync
        def _(sp_):
            for dst, src in small:
                sp_.dma_start(dst, src).then_inc(sem("small_in"), 16)
            for b in range(3):
                sp_.dma_start(aring[b], ada_k[:, :, b * 512:(b + 1) * 512])\
                    .then_inc(sem(f"ada_in{b % 3}"), 16)
            for b in range(3, NAB):
                sp_.wait_ge(sem("ada_used"), b - 2)
                sp_.dma_start(aring[b % 3], ada_k[:, :, b * 512:(b + 1) * 512])\
                    .then_inc(sem(f"ada_in{b % 3}"), 16)
            for t in range(NT):
                src = x_t[t] if t < NL else ctx_t[t - NL]
                sp_.dma_start(xall[:, t, :], src).then_inc(sem(f"tile_in{t // 2}"), 16)
            sp_.dma_start(taps[:], taps_k).then_inc(sem("taps_in"), 16)
            sp_.dma_start(rw[:], rw_k).then_inc(sem("taps_in"), 16)
            sp_.dma_start(wring[0][:, :, 0:NGATE], w_k[:, :, OFF_GATE:OFF_GATE + NGATE]).then_inc(sem("w_in0"), 16)
            for m in range(NM):
                s = (m + 1) % NW
                if m + 1 >= NW:
                    sp_.wait_ge(sem("w_used"), m + 1 - NW + 1)
                col = tiles[m][0]
                sp_.dma_start(wring[s], w_k[:, :, col:col + P]).then_inc(sem(f"w_in{s}"), 16)
                if NW - 1 <= m < NW + 1:
                    late_load(m - NW + 1)
                elif 2 <= m - NW - 1 < NLB:
                    b = m - NW - 1
                    sp_.wait_ge(sem("aux_used"), n_aux(b - 2 + LATE - 1) + 1)
                    late_load(b)
            for zh in range(2):
                if zh == 0:
                    sp_.wait_ge(sem("w_used"), NM + 1)
                else:
                    sp_.wait_ge(sem("zps"), NL)
                sp_.dma_start(wz, w_k[:, :, OFF_Z + zh * 512:OFF_Z + (zh + 1) * 512]).then_inc(sem("wz_in"), 16)
            sp_scan(sp_)
            sp_tail(sp_)

        def arrived(eng, m):
            s = (m + 1) % NW
            eng.wait_ge(sem(f"w_in{s}"), 16 * ((m + 1) // NW + 1))

        @block.gpsimd
        def _(pool):
            nc.gpsimd.memset(ident[:], 0.0).then_inc(sem("c0"), 1)
            nc.gpsimd.memset(ones[:], 1.0).then_inc(sem("c0"), 1)
            nc.gpsimd.memset(neg_mask[:], 0.0).then_inc(sem("c0"), 1)
            nc.gpsimd.memset(cum_mask[:], 1.0).then_inc(sem("c0"), 1)
            nc.gpsimd.memset(lvl_mask[:], 1.0).then_inc(sem("c0"), 1)
            pool.wait_ge(sem("c0"), 5)
            nc.gpsimd.affine_select(out=ident[:], in_=ident[:], compare_op=ALU.not_equal, fill=1.0,
                                    base=0, pattern=[[-1, P]], channel_multiplier=1).then_inc(sem("c1"), 1)
            for d, s in ((0, 1), (1, -1)):
                nc.gpsimd.affine_select(out=neg_mask[:, d, :], in_=neg_mask[:, d, :], compare_op=ALU.is_ge,
                                        fill=NEG, base=0, pattern=[[s, P]], channel_multiplier=-s)\
                    .then_inc(sem("c1"), 1)
                nc.gpsimd.affine_select(out=cum_mask[:, d, :], in_=cum_mask[:, d, :], compare_op=ALU.is_ge,
                                        fill=0.0, base=0, pattern=[[s, P]], channel_multiplier=-s)\
                    .then_inc(sem("c1"), 1)
            n = 5
            for d in range(2):
                for lv in range(7):
                    s = 1 << lv
                    m = lvl_mask[:, d, lv, :].rearrange("p (b s) -> p b s", s=2 * s)
                    nb = P // (2 * s)
                    un = m[:, :, s:2 * s] if d == 0 else m[:, :, 0:s]
                    us = m[:, :, 0:s] if d == 0 else m[:, :, s:2 * s]
                    nc.gpsimd.memset(un, 0.0).then_inc(sem("c1"), 1)
                    n += 1
                    lo = s if d == 0 else 0
                    nc.gpsimd.affine_select(out=us, in_=us, compare_op=ALU.is_ge, fill=0.0, base=-lo,
                                            pattern=[[-2 * s, nb], [0, s]], channel_multiplier=1)\
                        .then_inc(sem("c1"), 1)
                    n += 1
                    pool.wait_ge(sem("c1"), n)
                    nc.gpsimd.affine_select(out=us, in_=us, compare_op=ALU.is_ge, fill=0.0, base=lo + s - 1,
                                            pattern=[[2 * s, nb], [0, s]], channel_multiplier=-1)\
                        .then_inc(sem("c1"), 1)
                    n += 1
            assert n == N_C1[0]
            for m in range(NM):
                kind, i, has_ctx = tiles[m][1:]
                if kind in "kq":
                    n_kq = i + 1 if kind == "k" else DN_H + i + 1
                    dst = {"k": kT, "q": qT}[kind][:, i, :]
                    pool.wait_ge(sem("nrm_rec"), n_kq)
                    nc.gpsimd.tensor_tensor(dst, dst, ctmp[:, 0:TA if has_ctx else T], ALU.mult)\
                        .then_inc(sem("nrm_mul"), 1)
            pool_scan(pool)
            pool_tail(pool)

        NXG = (NL + 3) // 4 + 1
        XG = [(0, 4), (4, 4), (8, 2)]
        assert NL == 8 and NC == 2

        def parts_of(m):
            return [(0, 512), (512, 512)] + ([(1024, TC)] if tiles[m][3] else [])

        def n_kq(m):
            return sum(tl[1] in "kq" for tl in tiles[:m])

        @block.tensor
        def _(pe):
            pe.wait_ge(sem("c1"), N_C1[0])
            pe.wait_ge(sem("small_in"), 16 * len(small))
            nc.tensor.transpose(ps[0][:, 0:NV], vrows, ident[0:NV, 0:NV]).then_inc(sem("vT"), 1)
            nc.tensor.matmul(ps[1][:, 0:56], ones[0:1, :], srow[0:1, :], start=True, stop=True)\
                .then_inc(sem("vT"), 1)
            pe.wait_ge(sem("silu_c"), 2)
            for b in range(NAB):
                pe.wait_ge(sem(f"ada_in{b % 3}"), 16 * (b // 3 + 1))
                if b >= 2:
                    pe.wait_ge(sem("mrow"), b - 1)
                for k in range(KD):
                    last = nc.tensor.matmul(ps[2 + b % 2][0:2, :], silu_c[:, k, :], aring[b % 3][:, k, :],
                                            start=(k == 0), stop=(k == KD - 1))
                last.then_inc(sem("ada_used"), 1)
            pe.wait_ge(sem("mrow"), NAB)
            pe.wait_ge(sem("vcols"), 2)
            for j in range(2 * KD):
                last = nc.tensor.transpose(ps[1][:, 2 * j:2 * j + 2], mrow[:, j * P:(j + 1) * P], ident[0:2, 0:2])
            last.then_inc(sem("modT"), 1)
            n = 0
            for t0, nt in XG:
                pe.wait_ge(sem("xn"), t0 + nt)
                for k in range(KD):
                    if n >= 4:
                        pe.wait_ge(sem("hT"), n - 3)
                    for i in range(nt):
                        last = nc.tensor.transpose(ps[4 + n % 4][:, i * P:(i + 1) * P],
                                                   xall[:, t0 + i, k * P:(k + 1) * P], ident[:])
                    last.then_inc(sem("xT"), 1)
                    n += 1
            pe.wait_ge(sem("hT"), n)
            pe.wait_ge(sem("w_in0"), 16)
            for t in range(NT):
                for k in range(KD):
                    last = nc.tensor.matmul(ps[3][:, t * NGATE:(t + 1) * NGATE], hT[:, k, t * P:(t + 1) * P],
                                            wring[0][:, k, 0:NGATE], start=(k == 0), stop=(k == KD - 1))
            last.then_inc(sem("w_used"), 1)
            aux = 0
            for m in range(NM + 1):
                if m < NM:
                    arrived(pe, m)
                    if m >= 2:
                        pe.wait_ge(sem("cin"), m - 1)
                    if m == 1:
                        pe.wait_ge(sem("graw"), 1)
                    for gi, (o, w) in enumerate(parts_of(m)):
                        for k in range(KD):
                            last = nc.tensor.matmul(ps[3 * (m % 2) + gi][:, 0:w], wring[(m + 1) % NW][:, k, :],
                                                    hT[:, k, o:o + w], start=(k == 0), stop=(k == KD - 1))
                    last.then_inc(sem("w_used"), 1)
                if m == 0:
                    pe.wait_ge(sem("logg"), 1)
                    for d in range(2):
                        nc.tensor.matmul(ps[7][:, d * NT * GD:(d + 1) * NT * GD], cum_mask[:, d, :],
                                         ga[:, :, d, :], start=True, stop=True)
                    nc.tensor.matmul(ps[7][:, 240:480], ones[:], ga[:].rearrange("p t d g -> p (t d g)"),
                                     start=True, stop=True).then_inc(sem("Gps"), 1)
                if late_before(m + 1) > late_before(m):
                    b = m - LATE
                    pe.wait_ge(sem("late"), b + 1)
                    pe.wait_ge(sem("aux_used"), aux - 1)
                    for q in range(4):
                        last = nc.tensor.matmul(ps[6 + aux % 2][:, q:q + 1], lring[b % 2][:, 0, q * P:(q + 1) * P],
                                                ones[:, 0:1], start=True, stop=True)
                    last.then_inc(sem("aux"), 1)
                    aux += 1
                if m >= 1:
                    kind, i, has_ctx = tiles[m - 1][1:]
                    pe.wait_ge(sem("silu"), m)
                    if m == 1:
                        pe.wait_ge(sem("Gev"), 2)
                    if kind in "kq":
                        for o, w in parts_of(m - 1):
                            if aux >= 2:
                                pe.wait_ge(sem("aux_used"), aux - 1)
                            nc.tensor.matmul(ps[6 + aux % 2][:, 0:w], ones[:], ctmp[:, o:o + w],
                                             start=True, stop=True).then_inc(sem("aux"), 1)
                            aux += 1
                    elif kind in "vxB":
                        src = BT[:, i, :] if kind == "B" else ctmp
                        for t0, nt in XG:
                            if aux >= 2:
                                pe.wait_ge(sem("aux_used"), aux - 1)
                            for q in range(nt):
                                last = nc.tensor.transpose(ps[6 + aux % 2][:, q * P:(q + 1) * P],
                                                           src[:, (t0 + q) * P:(t0 + q + 1) * P], ident[:])
                            last.then_inc(sem("aux"), 1)
                            aux += 1
            pe.wait_ge(sem("cin"), NM)
            for zb in range(2 * NL):
                if zb % NL == 0:
                    pe.wait_ge(sem("wz_in"), 16 * (zb // NL + 1))
                if zb >= 4:
                    pe.wait_ge(sem("zsb"), zb - 3)
                t = zb % NL
                for k in range(KD):
                    last = nc.tensor.matmul(ps[zb % 4][:], hT[:, k, t * P:(t + 1) * P], wz[:, k, :],
                                            start=(k == 0), stop=(k == KD - 1))
                last.then_inc(sem("zps"), 1)
            pe_scan(pe)
            pe_tail(pe)

        @block.scalar
        def _(act):
            act.wait_ge(sem("vcols"), 2)
            for j, v0 in enumerate((V_C, V_CC)):
                nc.scalar.activation(silu_c[:, :, j], vcols[:, v0:v0 + KD], ACT.Silu).then_inc(sem("silu_c"), 1)
            for t in range(NT):
                act.wait_ge(sem(f"tile_in{t // 2}"), 32)
                nc.scalar.activation(hflat[:, t * D:(t + 1) * D], xall[:, t, :], ACT.Square,
                                     accum_out=ssq[:, t:t + 1]).then_inc(sem("ssq"), 1)
                act.wait_ge(sem("ssq"), t + 1)
                nc.scalar.activation(rstd[:, t:t + 1], ssq[:, t:t + 1], ACT.Sqrt, scale=1.0 / D, bias=eps_d[:])\
                    .then_inc(sem("rms"), 1)
            act.wait_ge(sem("gain1"), 1)
            n = 0
            for t0, nt in XG:
                j = 0 if t0 < NL else 1
                for k in range(KD):
                    act.wait_ge(sem("xT"), n + 1)
                    nc.scalar.activation(hT[:, k, t0 * P:(t0 + nt) * P], ps[4 + n % 4][:, 0:nt * P], ACT.Identity,
                                         bias=mods[:, k, j:j + 1], scale=gain1[:, k, j:j + 1])\
                        .then_inc(sem("hT"), 1)
                    n += 1
            act.wait_ge(sem("gabs"), 2)
            nc.scalar.activation(beta_f, beta_f, ACT.Exp).then_inc(sem("gexp"), 1)
            nc.scalar.activation(gb[:], gb[:], ACT.Exp).then_inc(sem("gexp"), 1)
            nc.scalar.activation(gneg[:], sbc[:, 24:48].rearrange("p (d g) -> p d g", d=2), ACT.Exp)\
                .then_inc(sem("gexp"), 1)
            act.wait_ge(sem("gln"), 1)
            nc.scalar.activation(eG[:], G[:], ACT.Ln).then_inc(sem("gln_out"), 1)
            act.wait_ge(sem("Gev"), 3)
            nc.scalar.activation(eG[:], G[:], ACT.Exp).then_inc(sem("eG"), 1)
            nc.scalar.activation(eGt[:], gb[:], ACT.Exp).then_inc(sem("eG"), 1)
            nc.scalar.activation(wtail[:], ga[:], ACT.Exp).then_inc(sem("eG"), 1)

            aux = 0
            for m in range(NM + 1):
                if late_before(m + 1) > late_before(m):
                    act.wait_ge(sem("aux"), aux + 1)
                    j = 2 * KD + 4 * (m - LATE)
                    nc.scalar.activation(mods[:, j:j + 4, 0], ps[6 + aux % 2][:, 0:4], ACT.Copy)\
                        .then_inc(sem("aux_used"), 1)
                    aux += 1
                if m >= 1:
                    mm = m - 1
                    col, kind, i, has_ctx = tiles[mm]
                    w = TA if has_ctx else T
                    act.wait_ge(sem("conv"), mm + 1)
                    if n_kq(mm):
                        act.wait_ge(sem("nrm_mul"), n_kq(mm))
                    dst = ctmp[:, 0:w] if kind in "vx" else {"k": kT, "q": qT, "B": BT, "C": CT}[kind][:, i, 0:w]
                    bcol = vcols[:, V_CB + col // P:V_CB + col // P + 1]
                    ins = nc.scalar.activation(dst, cacc[mm % 2][:, 0:w], ACT.Silu, bias=bcol)
                    if kind in "kq":
                        ins.then_inc(sem("silu_kq"), 1)
                        act.wait_ge(sem("silu_kq"), n_kq(mm) + 1)
                        ins = nc.scalar.activation(ctmp[:, 0:w], dst, ACT.Square)
                    ins.then_inc(sem("silu"), 1)
                    if kind in "kq":
                        f = 1.0 if kind == "k" else float(DK)
                        eb = eps1 if kind == "k" else eps_q
                        for o, ww in parts_of(mm):
                            act.wait_ge(sem("aux"), aux + 1)
                            nc.scalar.activation(ctmp[:, o:o + ww], ps[6 + aux % 2][:, 0:ww], ACT.Sqrt, scale=f,
                                                 bias=eb[:]).then_inc(sem("aux_used"), 1)
                            aux += 1
                    elif kind in "vxB":
                        for t0, nt in XG:
                            act.wait_ge(sem("aux"), aux + 1)
                            dstt = {"v": vtok, "x": xtok, "B": Btok}[kind]
                            nc.scalar.activation(dstt[:, t0:t0 + nt, i * P:(i + 1) * P],
                                                 ps[6 + aux % 2][:, 0:nt * P].rearrange("p (t c) -> p t c", c=P),
                                                 ACT.Copy).then_inc(sem("aux_used"), 1)
                            aux += 1
                if m < NM:
                    act.wait_ge(sem("w_used"), m + 2)
                    if m == 0:
                        act.wait_ge(sem("pad"), 4)
                    if m >= 2:
                        act.wait_ge(sem("conv"), m - 1)
                    for gi in range(2):
                        last = nc.scalar.activation(
                            cin_l[m % 2][:, 1 + 8 * gi:9 + 8 * gi, 1:1 + GW],
                            ps[3 * (m % 2) + gi][:].rearrange("p (r c) -> p r c", c=GW), ACT.Copy)
                    if tiles[m][3]:
                        last = nc.scalar.activation(cin_c[m % 2][:, 1:1 + TC], ps[3 * (m % 2) + 2][:, 0:TC],
                                                    ACT.Copy)
                    last.then_inc(sem("cin"), 1)
            for zb in range(2 * NL):
                act.wait_ge(sem("zps"), zb + 1)
                if zb >= 2:
                    act.wait_ge(sem(f"z_out{zb % 2}"), 16 * (zb // 2))
                nc.scalar.activation(zst[zb % 2], ps[zb % 4][:], ACT.Silu).then_inc(sem("zsb"), 1)
                act.wait_ge(sem("zsb"), zb + 1)
                act.dma_start(z_dram[zb % NL, :, (zb // NL) * 512:(zb // NL + 1) * 512], zst[zb % 2])\
                    .then_inc(sem(f"z_out{zb % 2}"), 16)
            act_scan(act)
            act_tail(act)

        @block.vector
        def _(dve):
            chain = [0]

            def link(ins):
                chain[0] += 1
                ins.then_inc(sem("dve_chain"), 1)
                dve.wait_ge(sem("dve_chain"), chain[0])

            v = nc.vector
            v.memset(eps_d[:], EPS)
            v.memset(eps1[:], EPS)
            v.memset(eps_q[:], EPS * DK)
            for i in range(2):
                v.memset(cin_l[i], 0.0).then_inc(sem("pad"), 1)
                v.memset(cin_c[i], 0.0).then_inc(sem("pad"), 1)
            dve.wait_ge(sem("vT"), 2)
            v.tensor_copy(vcols[:], ps[0][:, 0:NV]).then_inc(sem("vcols"), 1)
            v.tensor_copy(sbc[:], ps[1][:, 0:56]).then_inc(sem("vcols"), 1)
            for b in range(NAB):
                dve.wait_ge(sem("ada_used"), b + 1)
                v.tensor_copy(mrow[:, b * 512:(b + 1) * 512], ps[2 + b % 2][0:2, :]).then_inc(sem("mrow"), 1)
            dve.wait_ge(sem("vcols"), 2)
            dve.wait_ge(sem("modT"), 1)
            link(v.tensor_tensor(mods[:, 0:2 * KD, :], ps[1][:, 0:4 * KD].rearrange("p (j w) -> p j w", w=2),
                                 vcols[:, V_AB:V_AB + 2 * KD].unsqueeze(2).to_broadcast([P, 2 * KD, 2]), ALU.add))
            v.scalar_tensor_tensor(gain1[:], mods[:, KD:2 * KD, :], 1.0,
                                   vcols[:, V_NG:V_NG + KD].unsqueeze(2).to_broadcast([P, KD, 2]),
                                   ALU.add, ALU.mult).then_inc(sem("gain1"), 1)
            for t in range(NT):
                dve.wait_ge(sem("rms"), t + 1)
                link(v.reciprocal(rstd[:, t:t + 1], rstd[:, t:t + 1]))
                v.tensor_scalar(xall[:, t, :], xall[:, t, :], rstd[:, t:t + 1], None, ALU.mult)\
                    .then_inc(sem("xn"), 1)
            dve.wait_ge(sem("w_used"), 1)
            v.tensor_copy(gates[:], ps[3][:, 0:NT * NGATE].rearrange("p (t g) -> p t g", g=NGATE))\
                .then_inc(sem("graw"), 1)
            dve.wait_ge(sem("graw"), 1)
            v.scalar_tensor_tensor(beta_f, gates[:, :, 0:2 * DN_H], -1.0, gates[:, :, 0:2 * DN_H],
                                   ALU.mult, ALU.min).then_inc(sem("gabs"), 1)
            for d in range(2):
                a0, t0 = 2 * DN_H + d * DN_H, 4 * DN_H + d * SSM_H
                for g0, n, c0 in ((0, DN_H, a0), (DN_H, SSM_H, t0)):
                    ins = v.tensor_tensor(ga[:, :, d, g0:g0 + n], gates[:, :, c0:c0 + n],
                                          sbc[:, d * GD + g0:d * GD + g0 + n].unsqueeze(1).to_broadcast([P, NT, n]),
                                          ALU.add)
            link(ins)
            gaf, gbf, Gf, eGf, eGtf, spf = (a[:].rearrange("p t d g -> p (t d g)") for a in (ga, gb, G, eG, eGt, sp))
            v.scalar_tensor_tensor(gbf, gaf, -1.0, gaf, ALU.mult, ALU.min).then_inc(sem("gabs"), 1)
            dve.wait_ge(sem("gexp"), 3)
            link(v.scalar_tensor_tensor(gates[:, :, 0:2 * DN_H], gates[:, :, 0:2 * DN_H], 0.0, beta_f,
                                        ALU.is_ge, ALU.max))
            link(v.tensor_scalar(beta_f, beta_f, 1.0, None, ALU.add))
            link(v.reciprocal(beta_f, beta_f))
            link(v.tensor_tensor(beta_f, beta_f, gates[:, :, 0:2 * DN_H], ALU.mult))
            v.tensor_scalar(Gf, gbf, 1.0, None, ALU.add).then_inc(sem("gln"), 1)
            dve.wait_ge(sem("gln_out"), 1)
            link(v.tensor_scalar(Gf, Gf, -1.0, None, ALU.add))
            link(v.tensor_scalar(eGtf, Gf, 0.0, None, ALU.is_equal))
            v.tensor_tensor(Gf, Gf, eGtf, ALU.add)
            link(v.tensor_tensor(eGf, eGf, eGtf, ALU.add))
            link(v.reciprocal(Gf, Gf))
            link(v.tensor_tensor(Gf, Gf, eGf, ALU.mult))
            link(v.tensor_tensor(Gf, Gf, gbf, ALU.mult))
            link(v.scalar_tensor_tensor(spf, gaf, 0.0, Gf, ALU.max, ALU.add))
            v.scalar_tensor_tensor(ga[:].rearrange("p t d g -> p t (d g)"), sp[:].rearrange("p t d g -> p t (d g)"),
                                   -1.0, gneg[:].rearrange("p d g -> p (d g)").unsqueeze(1)
                                   .to_broadcast([P, NT, 2 * GD]), ALU.mult, ALU.mult).then_inc(sem("logg"), 1)
            dve.wait_ge(sem("Gps"), 1)
            v.tensor_copy(G[:], ps[7][:, 0:240].rearrange("p (d t g) -> p t d g", d=2, g=GD)).then_inc(sem("Gev"), 1)
            v.tensor_copy(gbf, ps[7][:, 240:480]).then_inc(sem("Gev"), 1)
            dve.wait_ge(sem("Gev"), 2)
            v.tensor_tensor(gaf, gbf, Gf, ALU.subtract).then_inc(sem("Gev"), 1)
            dve.wait_ge(sem("eG"), 3)
            v.tensor_tensor(wtail[:, :, :, 0:DN_H], wtail[:, :, :, 0:DN_H], beta[:], ALU.mult).then_inc(sem("wtail"), 1)
            v.tensor_tensor(wtail[:, :, :, DN_H:GD], wtail[:, :, :, DN_H:GD], sp[:, :, :, DN_H:GD], ALU.mult)\
                .then_inc(sem("wtail"), 1)

            dve.wait_ge(sem("taps_in"), 32)
            for m in range(NM + 1):
                if m >= 1 and tiles[m - 1][1] in "kq":
                    w = TA if tiles[m - 1][3] else T
                    dve.wait_ge(sem("aux_used"), n_aux(m))
                    v.reciprocal(ctmp[:, 0:w], ctmp[:, 0:w]).then_inc(sem("nrm_rec"), 1)
                if m == NM:
                    break
                col, kind, i, has_ctx = tiles[m]
                tp = taps[:, col // P, :]
                acc = cacc[m % 2]
                accg = acc[:, 0:T].rearrange("p (r c) -> p r c", c=GW)
                dve.wait_ge(sem("cin"), m + 1)
                if m >= 2:
                    dve.wait_ge(sem("silu"), m - 1)
                if has_ctx:
                    link(v.tensor_scalar(acc[:, T:TA], cin_c[m % 2][:, 0:TC], tp[:, 3:4], None, ALU.mult))
                    for j in (1, 2):
                        link(v.scalar_tensor_tensor(acc[:, T:TA], cin_c[m % 2][:, j:j + TC], tp[:, 3 + j:4 + j],
                                                    acc[:, T:TA], ALU.mult, ALU.add))
                link(v.tensor_scalar(accg, cin_l[m % 2][:, 0:GR, 0:GW], tp[:, 0:1], None, ALU.mult))
                for j in range(1, 9):
                    ins = v.scalar_tensor_tensor(accg, cin_l[m % 2][:, j // 3:j // 3 + GR, j % 3:j % 3 + GW],
                                                 tp[:, j:j + 1], accg, ALU.mult, ALU.add)
                    if j < 8:
                        link(ins)
                ins.then_inc(sem("conv"), 1)
                b = m - LATE + 2
                if 0 <= b < NLB:
                    blk = lring[b % 2]
                    dve.wait_ge(sem(f"late_in{b % 2}"), 16 * (b // 2 + 1))
                    link(v.tensor_scalar(blk[:, 0, :], blk[:, 0, :], silu_c[:, 0, 0:1], None, ALU.mult))
                    for k in range(1, KD):
                        ins = v.scalar_tensor_tensor(blk[:, 0, :], blk[:, k, :], silu_c[:, k, 0:1], blk[:, 0, :],
                                                     ALU.mult, ALU.add)
                        if k < KD - 1:
                            link(ins)
                    ins.then_inc(sem("late"), 1)
            dve_scan(dve, link)
            dve_tail(dve, link)


def kernel(**inputs):
    import concourse.bacc as bacc
    import numpy as np
    from concourse.bass_utils import run_bass_kernel_spmd

    names = ["x", "c", "ctx", "c_ctx", "ada_w", "ada_b", "norm_g", "w_in", "conv_w", "conv_b", "dn_A_log",
             "dn_dt_bias", "dn_norm_g", "ssm_A_log", "ssm_dt_bias", "ssm_D", "ssm_norm_g", "w_out", "router_w",
             "exp_w_gate", "exp_w_up", "exp_w_down"]
    nc = bacc.Bacc("TRN2", target_bir_lowering=False, num_devices=1)
    arrays = {n: np.ascontiguousarray(inputs[n]) for n in names}
    args = [nc.dram_tensor(n, arrays[n].shape, mybir.dt.from_np(arrays[n].dtype), kind="ExternalInput").ap()
            for n in names]
    out = nc.dram_tensor("out", arrays["x"].shape, F32, kind="ExternalOutput").ap()
    hybrid_block(nc, *args, out)
    r = run_bass_kernel_spmd(nc, [arrays], core_ids=[0])
    return r.results[0]["out"]
```

```python
from contextlib import ExitStack

import concourse.bass as bass
from concourse import mybir

P = 128
F32 = mybir.dt.float32
U32 = mybir.dt.uint32
ALU = mybir.AluOpType
ACT = mybir.ActivationFunctionType
AX = mybir.AxisListType
EPS = 1e-6
NEG = -1.0e30


def hybrid_block(nc, x, c, ctx, c_ctx, ada_w, ada_b, norm_g, w_in, conv_w, conv_b, dn_A_log, dn_dt_bias,
                 dn_norm_g, ssm_A_log, ssm_dt_bias, ssm_D, ssm_norm_g, w_out, router_w,
                 exp_w_gate, exp_w_up, exp_w_down, out):
    T, D = x.shape[1:]
    TC = ctx.shape[1]
    DN_H, DK, SSM_H, SSM_P, SSM_G, GW = 4, 128, 8, 64, 2, 64
    KD = D // P
    NL, NC = T // P, TC // P
    NT = NL + NC
    TA = T + TC
    E_N, F = exp_w_gate.shape[1], exp_w_gate.shape[3]
    KF = F // P
    CAP = 2 * T // E_N
    GR = T // GW
    QK = DN_H * DK
    DI = SSM_H * SSM_P
    CONV_CH = conv_w.shape[1]
    HPG = SSM_H // SSM_G
    OFF_Q, OFF_K, OFF_V, OFF_X = 0, QK, 2 * QK, 3 * QK
    OFF_B, OFF_C = OFF_X + DI, OFF_X + DI + SSM_G * P
    OFF_Z = CONV_CH
    OFF_GATE = OFF_Z + QK + DI
    NGATE = w_in.shape[2] - OFF_GATE
    GD = DN_H + SSM_H
    assert CAP == P and NGATE == 2 * (2 * DN_H + SSM_H) and D == 8 * P and QK == 512 and DI == 512

    z_dram = nc.dram_tensor("z_dram", (NL, P, QK + DI), F32, kind="Internal").ap()
    scan_dram = nc.dram_tensor("scan_dram", (2, NL, P, QK + DI), F32, kind="Internal").ap()
    h2_dram = nc.dram_tensor("h2_dram", (T, D), F32, kind="Internal").ap()
    y_dram = nc.dram_tensor("y_dram", (T, D), F32, kind="Internal").ap()

    with ExitStack() as es:
        def sb(name, shape, dt=F32):
            return es.enter_context(nc.sbuf_tensor(name, shape, dt))

        sems = {}

        def sem(name):
            if name not in sems:
                sems[name] = es.enter_context(nc.semaphore(name))
            return sems[name]

        ident = sb("ident", [P, P])
        ones = sb("ones", [P, P])
        cum_mask = sb("cum_mask", [P, 2, P])
        neg_mask = sb("neg_mask", [P, 2, P])
        lvl_mask = sb("lvl_mask", [P, 2, 7, P])
        NV = 2 * KD + 6 * KD + 4 * KD + CONV_CH // P + 1 + DI // P
        vcols = sb("vcols", [P, NV])
        V_C, V_CC, V_AB, V_NG = 0, KD, 2 * KD, 8 * KD
        V_CB, V_DG, V_SG = 12 * KD, 12 * KD + CONV_CH // P, 12 * KD + CONV_CH // P + 1
        sbc = sb("sbc", [P, 56])
        silu_c = sb("silu_c", [P, KD, 2])
        mods = sb("mods", [P, 6 * KD, 2])
        gain1 = sb("gain1", [P, KD, 2])
        taps = sb("taps", [P, CONV_CH // P, 9])
        rw = sb("rw", [P, KD, E_N])
        ssq = sb("ssq", [P, NT])
        rstd = sb("rstd", [P, NT])
        gates = sb("gates", [P, NT, NGATE])
        beta = sb("beta", [P, NT, 2, DN_H])
        sp = sb("sp", [P, NT, 2, GD])
        ga = sb("ga", [P, NT, 2, GD])
        gb = sb("gb", [P, NT, 2, GD])
        gneg = sb("gneg", [P, 2, GD])
        G = sb("G", [P, NT, 2, GD])
        eG = sb("eG", [P, NT, 2, GD])
        eGt = sb("eGt", [P, NT, 2, GD])
        wtail = sb("wtail", [P, NT, 2, GD])

        arena = sb("arena", [P, 47700])
        at = [0]
        vrows = arena[0:NV, 24000:24000 + P]
        srow = arena[0:1, 24200:24256]

        def take(n):
            at[0] += n
            assert at[0] <= 47700, at[0]
            return arena[:, at[0] - n:at[0]]

        kT = take(DN_H * TA).rearrange("p (h t) -> p h t", h=DN_H)
        qT = take(DN_H * T).rearrange("p (h t) -> p h t", h=DN_H)
        BT = take(SSM_G * TA).rearrange("p (h t) -> p h t", h=SSM_G)
        CT = take(SSM_G * T).rearrange("p (h t) -> p h t", h=SSM_G)
        vtok = take(NT * QK).rearrange("p (t n) -> p t n", t=NT)
        XT0 = at[0]
        xtok = take(NT * DI).rearrange("p (t n) -> p t n", t=NT)
        Btok = take(NT * SSM_G * P).rearrange("p (t n) -> p t n", t=NT)
        W0 = at[0]
        xall = arena[:, 0:NT * D].rearrange("p (t n) -> p t n", t=NT)
        hT = take(KD * TA).rearrange("p (k t) -> p k t", k=KD)
        ABLK = 4096
        aring = [arena[:, 11000 + i * ABLK:11000 + (i + 1) * ABLK].rearrange("p (k n) -> p k n", k=KD)
                 for i in range(3)]
        lring = [arena[:, o:o + ABLK].rearrange("p (k n) -> p k n", k=KD) for o in (DN_H * TA, XT0)]
        NW = 4
        wring_all = take(NW * KD * P)
        wring = [wring_all[:, i * KD * P:(i + 1) * KD * P].rearrange("p (k n) -> p k n", k=KD) for i in range(NW)]
        wz0 = wring_all.rearrange("p (s k n) -> p s k n", s=NW, k=KD)
        wz1 = arena[:, at[0]:at[0] + KD * 512].rearrange("p (k n) -> p k n", k=KD)
        zst = [arena[:, at[0] + KD * 512 + i * 512:at[0] + KD * 512 + (i + 1) * 512] for i in range(2)]
        GP = (GR + 2) * (GW + 2)
        cin_l = [take(GP).rearrange("p (r c) -> p r c", c=GW + 2) for _ in range(2)]
        cin_c = [take(TC + 2) for _ in range(2)]
        mrow = arena[0:2, at[0]:at[0] + 2 * D]
        cacc = [take(TA) for _ in range(2)]
        ctmp = take(TA)
        assert NT * 2 * 5 * GD <= TA
        pack = ctmp[:, 0:NT * 2 * 5 * GD].rearrange("p (t d q g) -> p t d q g", t=NT, d=2, q=5)
        PACK0 = at[0] - TA

        ps = [es.enter_context(nc.psum_tensor(f"ps{i}", [P, 512], F32)) for i in range(8)]

        x_t = x.rearrange("a (t p) d -> (a t) p d", p=P)
        ctx_t = ctx.rearrange("a (t p) d -> (a t) p d", p=P)
        ada_k = ada_w.rearrange("a (k p) n -> (a p) k n", p=P)
        w_k = w_in.rearrange("a (k p) n -> (a p) k n", p=P)
        rw_k = router_w.rearrange("a (k p) n -> (a p) k n", p=P)
        taps_k = conv_w.rearrange("a (m p) i j -> (a p) m (i j)", p=P)
        NAB = 2 * D // 512
        NLB = 4 * D // 512
        LATE = 4

        tiles = []
        for i in range(DN_H):
            tiles.append((OFF_K + i * P, "k", i, True))
        for i in range(SSM_G):
            tiles.append((OFF_B + i * P, "B", i, True))
        for i in range(QK // P):
            tiles.append((OFF_V + i * P, "v", i, True))
        for i in range(DI // P):
            tiles.append((OFF_X + i * P, "x", i, True))
        for i in range(DN_H):
            tiles.append((OFF_Q + i * P, "q", i, False))
        for i in range(SSM_G):
            tiles.append((OFF_C + i * P, "C", i, False))
        NM = len(tiles)

        hflat = arena[:, W0:W0 + NT * D]
        beta_f = beta[:].rearrange("p t d h -> p t (d h)")
        eps_d, eps1, eps_q = sb("eps_d", [P, 1]), sb("eps1", [P, 1]), sb("eps_q", [P, 1])

        def n_aux(m):
            return late_before(m + 1) + sum((3 if tl[3] else 2) if tl[1] in "kq" else 3 if tl[1] in "vxB" else 0
                                            for tl in tiles[:m])

        def late_before(m):
            return min(max(m - LATE, 0), NLB)


        at[0] = W0
        L4 = DN_H * P
        kTs, kgT, qgT, E, AT, X, Y, T1, ktail, S = ([take(L4).rearrange("p (h n) -> p h n", h=DN_H)
                                                     for _ in range(2)] for _ in range(10))
        E8 = [take(SSM_H * P).rearrange("p (h n) -> p h n", h=SSM_H) for _ in range(2)]
        xdt, xw, hs = ([take(DI).rearrange("p (h n) -> p h n", h=SSM_H) for _ in range(2)] for _ in range(3))
        BTs, CTs, Bts = ([take(SSM_G * P).rearrange("p (g n) -> p g n", g=SSM_G) for _ in range(2)] for _ in range(3))
        ost = [take(QK + DI) for _ in range(2)]
        gs = [take(5 * GD).rearrange("p (q g) -> p q g", q=5) for _ in range(2)]
        zero = take(512)
        assert at[0] <= PACK0
        Q_G, Q_EG, Q_EGT, Q_WT, Q_W = range(5)
        bank = [{"A": ps[4 * d], "B": ps[4 * d + 1], "C": ps[4 * d + 2], "D": ps[4 * d + 3]} for d in range(2)]
        DN, SM = slice(0, DN_H), slice(DN_H, GD)
        LV = 7

        def heads(ap, h=DN_H):
            return ap.rearrange("p (h n) -> p h n", h=h)

        def flat(ap):
            return ap.rearrange("p h n -> p (h n)")

        def bc(ap, n):
            return ap.unsqueeze(2).to_broadcast([P, ap.shape[1], n])

        def bh(ap, h=DN_H):
            return ap.unsqueeze(1).to_broadcast([P, h, ap.shape[1]])

        def tile_of(lat, t, d):
            n = NL if lat else NC
            return t + (0 if lat else NL) if d == 0 else t * -1 + (n - 1 + (0 if lat else NL))

        def number(lat, t):
            return t + NC if lat else t

        def now(step):
            d, lat, t = step
            return number(lat, t) * 2 + (d + 1)

        def past(step):
            d, lat, t = step
            return number(lat, t) * 2 + (d - 1)

        def now_lat(step):
            return step[2] * 2 + (step[0] + 1)

        def now_lv(step, per, lv):
            d, lat, t = step
            return number(lat, t) * (2 * per) + (d * per + lv)

        def started(step):
            return step[2] * 2 + (step[0] + 1)

        D_LAT = {"sqk": 0, "g8a": 1, "g8b": 2, "sc": 3, "yoff": 4, "ydiag": 5, "st": 6, "kv": 7}
        D_CTX = {"st": 0, "kv": 1}

        def d_before(step, use=None):
            d, lat, t = step
            if lat:
                return t * len(D_LAT) + (NC * len(D_CTX) + (D_LAT[use] if use else 0))
            return t * len(D_CTX) + (D_CTX[use] if use else 0)

        def turns(eng, turn):
            turn(None, None, (0, False, 0))
            turn((0, False, 0), None, (1, False, 0))
            for t in range(1, NC):
                turn((1, False, t - 1), (0, False, t - 1), (0, False, t))
                turn((0, False, t), (1, False, t - 1), (1, False, t))
            turn((1, False, NC - 1), (0, False, NC - 1), (0, True, 0))
            turn((0, True, 0), (1, False, NC - 1), (1, True, 0))
            with eng.Fori(0, NL - 1) as t:
                turn((1, True, t), (0, True, t), (0, True, t + 1))
                turn((0, True, t + 1), (1, True, t), (1, True, t + 1))
            turn((1, True, NL - 1), (0, True, NL - 1), None)
            turn(None, (1, True, NL - 1), None)

        def pe_scan(pe):
            mm, tr = nc.tensor.matmul, nc.tensor.transpose

            def rows(out, g):
                for h in range(g.shape[1]):
                    last = tr(out[:, h * P:(h + 1) * P], g[:, h:h + 1].to_broadcast([P, P]), ident[:])
                return last

            def per_head(out, lhsT, rhs):
                for h in range(DN_H):
                    last = mm(out[:, h * P:(h + 1) * P], lhsT[:, h, :], rhs[:, h, :], start=True, stop=True)
                return last

            def bank_d(step, use):
                d, lat, t = step
                if lat or t > 0 or D_CTX[use] > 0:
                    pe.wait_ge(sem(f"scan_dread{d}"), d_before(step, use))
                return bank[d]["D"]

            def g8(step, half):
                d = step[0]
                D = bank_d(step, ("g8a", "g8b")[half])
                rows(D, gs[d][:, Q_G, DN_H + 4 * half:DN_H + 4 * half + 4]).then_inc(sem(f"scan_dps{d}"), 1)

            def pre_a(step):
                d, lat, t = step
                pe.wait_ge(sem("scan_gs"), now(step))
                if lat or t > 0:
                    pe.wait_ge(sem("scan_yfin"), past(step))
                if lat:
                    pe.wait_ge(sem("scan_oc"), started(step))
                rows(bank[d]["A"], gs[d][:, Q_G, DN]).then_inc(sem("scan_grow"), 1)
                pe.wait_ge(sem("scan_kst"), now(step))
                if lat or t > 0:
                    pe.wait_ge(sem("scan_vnc"), past(step))
                per_head(bank[d]["B"], kTs[d], kTs[d]).then_inc(sem("scan_skk"), 1)

            def pre_b(step):
                d, lat, t = step
                if lat or t > 0:
                    pe.wait_ge(sem("scan_r"), past(step))
                for h in range(DN_H):
                    last = tr(bank[d]["C"][:, h * P:(h + 1) * P], kTs[d][:, h, :], ident[:])
                last.then_inc(sem("scan_ktr"), 1)
                if lat:
                    D = bank_d(step, "sqk")
                    ti = tile_of(lat, t, d)
                    for h in range(DN_H):
                        last = mm(D[:, h * P:(h + 1) * P], kTs[d][:, h, :],
                                  qT[:, h, bass.ds(ti * P, P)], start=True, stop=True)
                    last.then_inc(sem(f"scan_dps{d}"), 1)

            def pre_c(step):
                d = step[0]
                pe.wait_ge(sem("scan_y0"), now(step))
                pe.wait_ge(sem("scan_egrow"), now(step))
                pe.wait_ge(sem("scan_diff"), now(step))
                for h in range(DN_H):
                    last = tr(bank[d]["A"][:, h * P:(h + 1) * P], Y[d][:, h, :], ident[:])
                last.then_inc(sem("scan_xps"), 1)

            def level_a(step, lv):
                d = step[0]
                if lv == 1:
                    pe.wait_ge(sem("scan_x"), now(step))
                else:
                    pe.wait_ge(sem("scan_xn"), now_lv(step, LV - 2, lv - 1))
                per_head(bank[d]["B"], AT[d], X[d]).then_inc(sem("scan_t1"), 1)

            def level_b(step, lv):
                d = step[0]
                pe.wait_ge(sem("scan_t1m"), now_lv(step, LV - 1, lv))
                if lv > 1:
                    pe.wait_ge(sem("scan_y"), now_lv(step, LV - 2, lv - 1))
                l, r = (Y, T1) if lv < LV - 1 else (T1, Y)
                per_head(bank[d]["A"], l[d], r[d]).then_inc(sem("scan_xcx"), 1)

            def level_c(step, lv):
                d = step[0]
                pe.wait_ge(sem("scan_xn"), now_lv(step, LV - 2, lv))
                if lv == 1:
                    pe.wait_ge(sem("scan_ktail"), now(step))
                for h in range(DN_H):
                    last = tr(bank[d]["C"][:, h * P:(h + 1) * P], X[d][:, h, :], ident[:])
                last.then_inc(sem("scan_yps"), 1)

            def scores(step):
                d = step[0]
                D = bank_d(step, "sc")
                pe.wait_ge(sem("scan_cst"), now(step))
                for g in range(SSM_G):
                    last = mm(D[:, g * P:(g + 1) * P], BTs[d][:, g, :], CTs[d][:, g, :], start=True, stop=True)
                last.then_inc(sem(f"scan_dps{d}"), 1)

            def from_state(step):
                d = step[0]
                D = bank_d(step, "yoff")
                for g in range(SSM_G):
                    last = mm(D[:, g * 256:(g + 1) * 256], CTs[d][:, g, :],
                              flat(hs[d][:, g * HPG:(g + 1) * HPG, :]), start=True, stop=True)
                last.then_inc(sem(f"scan_dps{d}"), 1)

            def from_chunk(step):
                d = step[0]
                D = bank_d(step, "ydiag")
                pe.wait_ge(sem("scan_xst"), now(step))
                for h in range(SSM_H):
                    last = mm(D[:, h * SSM_P:(h + 1) * SSM_P], E8[d][:, h, :], xdt[d][:, h, :],
                              start=True, stop=True)
                last.then_inc(sem(f"scan_dps{d}"), 1)

            def to_state(step):
                d = step[0]
                D = bank_d(step, "st")
                pe.wait_ge(sem("scan_xst"), now(step))
                pe.wait_ge(sem("scan_cst"), now(step))
                for g in range(SSM_G):
                    last = mm(D[:, g * 256:(g + 1) * 256], Bts[d][:, g, :],
                              flat(xw[d][:, g * HPG:(g + 1) * HPG, :]), start=True, stop=True)
                last.then_inc(sem(f"scan_dps{d}"), 1)

            def post_a(step):
                d, lat, t = step
                pe.wait_ge(sem("scan_y"), now_lv(step, LV - 2, LV - 2))
                pe.wait_ge(sem("scan_kg"), now(step))
                if not lat and t == 0:
                    pe.wait_ge(sem("state0"), 4)
                per_head(bank[d]["C"], kgT[d], S[d]).then_inc(sem("scan_ks"), 1)

            def post_b(step):
                d = step[0]
                pe.wait_ge(sem("scan_r"), now(step))
                pe.wait_ge(sem("scan_yfin"), now(step))
                per_head(bank[d]["B"], Y[d], T1[d]).then_inc(sem("scan_vn"), 1)

            def post_c(step):
                d, lat, t = step
                pe.wait_ge(sem("scan_vnc"), now(step))
                if lat:
                    pe.wait_ge(sem("scan_qg"), now_lat(step))
                    for h in range(DN_H):
                        o = bank[d]["A"][:, h * P:(h + 1) * P]
                        mm(o, qgT[d][:, h, :], S[d][:, h, :], start=True, stop=False)
                        last = mm(o, E[d][:, h, :], X[d][:, h, :], start=False, stop=True)
                    last.then_inc(sem("scan_o"), 1)
                per_head(bank_d(step, "kv"), ktail[d], X[d]).then_inc(sem(f"scan_dps{d}"), 1)

            def turn(own, post, pre):
                own_lat = own and own[1]
                for lv in range(1, LV):
                    if own:
                        level_a(own, lv)
                    if lv == 1 and post:
                        post_a(post)
                    if lv == 2 and post:
                        post_b(post)
                    if lv == 3 and post:
                        post_c(post)
                    if lv == 4 and pre:
                        pre_a(pre)
                    if lv == 5 and pre:
                        pre_b(pre)
                    if own:
                        level_b(own, lv)
                    if lv == 1 and own_lat:
                        g8(own, 1)
                    if lv == 2 and own_lat:
                        scores(own)
                    if lv == 3 and own_lat:
                        from_state(own)
                    if lv == 4 and own_lat:
                        from_chunk(own)
                    if lv == 5 and own:
                        to_state(own)
                    if own and lv < LV - 1:
                        level_c(own, lv)
                    if lv == 6 and pre:
                        pre_c(pre)
                        if pre[1]:
                            g8(pre, 0)

            turns(pe, turn)

        def act_scan(act):
            a = nc.scalar.activation
            for i in range(2):
                act.wait_ge(sem(f"z_out{i}"), 16 * NL)
            for d in range(2):
                act.sem_inc(sem("scan_oc"), 1)

            def turn(own, post, pre):
                for lv in range(1, LV):
                    if own and lv < LV - 1:
                        d = own[0]
                        act.wait_ge(sem("scan_yps"), now_lv(own, LV - 2, lv))
                        a(flat(Y[d]), bank[d]["C"][:], ACT.Copy).then_inc(sem("scan_y"), 1)
                    if lv == 1 and own and own[1]:
                        act.wait_ge(sem(f"scan_dread{d}"), d_before(own, "g8b") + 1)
                        a(flat(E8[d]), flat(E8[d]), ACT.Exp).then_inc(sem("scan_e8"), 1)
                    if lv == 1 and post:
                        d = post[0]
                        act.wait_ge(sem("scan_vn"), now(post))
                        a(flat(X[d]), bank[d]["B"][:], ACT.Copy).then_inc(sem("scan_vnc"), 1)
                    if lv == 2 and post and post[1]:
                        d = post[0]
                        act.wait_ge(sem("scan_o"), now_lat(post))
                        act.wait_ge(sem(f"ost_out{d}"), post[2] * 16 + 16)
                        a(ost[d][:, 0:QK], bank[d]["A"][:], ACT.Copy).then_inc(sem("scan_oc"), 1)
                    if lv == 4 and pre:
                        d, lat, t = pre
                        act.wait_ge(sem("scan_diff"), now(pre))
                        a(flat(E[d]), flat(E[d]), ACT.Exp).then_inc(sem("scan_eexp"), 1)
                        if lat or t > 0:
                            act.wait_ge(sem("scan_ks"), past(pre))
                        a(flat(kgT[d]), bank[d]["A"][:], ACT.Exp).then_inc(sem("scan_egrow"), 1)
                    if lv == 6 and pre:
                        d = pre[0]
                        act.wait_ge(sem("scan_xps"), now(pre))
                        a(flat(X[d]), bank[d]["A"][:], ACT.Copy).then_inc(sem("scan_x"), 1)

            turns(act, turn)

        def dve_scan(dve, link):
            v = nc.vector

            dve.wait_ge(sem("zps"), 2 * NL)
            for i in range(2):
                dve.wait_ge(sem(f"z_out{i}"), 16 * NL)
            for d in range(2):
                v.memset(S[d], 0.0).then_inc(sem("state0"), 1)
                v.memset(hs[d], 0.0).then_inc(sem("state0"), 1)

            def d_full(step, use):
                dve.wait_ge(sem(f"scan_dps{step[0]}"), d_before(step, use) + 1)
                return bank[step[0]]["D"]

            def diff(d, out, src, g0):
                for h in range(4):
                    ins = v.scalar_tensor_tensor(out[:, h, :], src[:, h * P:(h + 1) * P],
                                                 gs[d][:, Q_G, g0 + h:g0 + h + 1], neg_mask[:, d, :],
                                                 ALU.subtract, ALU.min)
                return ins

            def g8(step, half):
                d = step[0]
                D = d_full(step, ("g8a", "g8b")[half])
                diff(d, E8[d][:, 4 * half:4 * half + 4, :], D, DN_H + 4 * half).then_inc(sem(f"scan_dread{d}"), 1)

            def pre_a(step):
                d = step[0]
                dve.wait_ge(sem("scan_grow"), now(step))
                if step[1]:
                    dve.wait_ge(sem("scan_oc"), started(step))
                diff(d, E[d], bank[d]["A"], 0).then_inc(sem("scan_diff"), 1)

            def pre_b(step):
                d = step[0]
                dve.wait_ge(sem("scan_skk"), now(step))
                dve.wait_ge(sem("scan_ebeta"), now(step))
                v.tensor_tensor(AT[d], heads(bank[d]["B"][:]), E[d], ALU.mult).then_inc(sem("scan_at"), 1)
                dve.wait_ge(sem("scan_at"), now(step))
                v.scalar_tensor_tensor(Y[d], AT[d], -1.0, bh(lvl_mask[:, 1 - d, 0, :]), ALU.mult, ALU.mult)\
                    .then_inc(sem("scan_y0a"), 1)

            def pre_c(step):
                d = step[0]
                dve.wait_ge(sem("scan_y0a"), now(step))
                v.tensor_tensor(Y[d], Y[d], bh(ident[:]), ALU.add).then_inc(sem("scan_y0"), 1)
                if step[1]:
                    D = d_full(step, "sqk")
                    v.tensor_tensor(E[d], heads(D[:]), E[d], ALU.mult).then_inc(sem(f"scan_dread{d}"), 1)

            def pre_d(step):
                d = step[0]
                dve.wait_ge(sem("scan_ktr"), now(step))
                v.tensor_tensor(ktail[d], heads(bank[d]["C"][:]), bc(gs[d][:, Q_WT, DN], P), ALU.mult)\
                    .then_inc(sem("scan_ktail"), 1)
                if step[1]:
                    g8(step, 0)

            def level_a(step, lv):
                d = step[0]
                dve.wait_ge(sem("scan_t1"), now_lv(step, LV - 1, lv))
                v.tensor_tensor(T1[d], heads(bank[d]["B"][:]), bh(lvl_mask[:, d, lv, :]), ALU.mult)\
                    .then_inc(sem("scan_t1m"), 1)

            def level_b(step, lv):
                d = step[0]
                dve.wait_ge(sem("scan_xcx"), now_lv(step, LV - 1, lv))
                if lv < LV - 1:
                    if lv > 1:
                        dve.wait_ge(sem("scan_xn"), now_lv(step, LV - 2, lv - 1))
                    v.tensor_tensor(X[d], X[d], heads(bank[d]["A"][:]), ALU.subtract).then_inc(sem("scan_xn"), 1)
                else:
                    v.tensor_tensor(Y[d], Y[d], heads(bank[d]["A"][:]), ALU.subtract).then_inc(sem("scan_yfin"), 1)

            def scores(step):
                d = step[0]
                D = d_full(step, "sc")
                dve.wait_ge(sem("scan_e8"), now_lat(step))
                for g in range(SSM_G):
                    hh = slice(g * HPG, (g + 1) * HPG)
                    ins = v.tensor_tensor(E8[d][:, hh, :], E8[d][:, hh, :], bh(D[:, g * P:(g + 1) * P], HPG), ALU.mult)
                ins.then_inc(sem(f"scan_dread{d}"), 1)

            def from_state(step):
                d, lat, t = step
                D = d_full(step, "yoff")
                dve.wait_ge(sem(f"ost_out{d}"), t * 16 + 16)
                v.tensor_tensor(heads(ost[d][:, QK:QK + DI], SSM_H), heads(D[:], SSM_H),
                                bc(gs[d][:, Q_EG, SM], SSM_P), ALU.mult).then_inc(sem(f"scan_dread{d}"), 1)

            def from_chunk(step):
                d = step[0]
                D = d_full(step, "ydiag")
                dve.wait_ge(sem(f"scan_dread{d}"), d_before(step, "yoff") + 1)
                v.tensor_tensor(ost[d][:, QK:QK + DI], ost[d][:, QK:QK + DI], D[:], ALU.add)\
                    .then_inc(sem(f"scan_dread{d}"), 1)

            def to_state(step):
                d = step[0]
                D = d_full(step, "st")
                dve.wait_ge(sem("scan_hg"), now(step))
                v.tensor_tensor(hs[d], hs[d], heads(D[:], SSM_H), ALU.add).then_inc(sem(f"scan_dread{d}"), 1)

            def post_a(step):
                d, lat, t = step
                dve.wait_ge(sem("scan_ks"), now(step))
                ti = tile_of(lat, t, d)
                v.tensor_tensor(flat(T1[d]), vtok[:, bass.ds(ti, 1), :].rearrange("p a n -> p (a n)"),
                                bank[d]["C"][:], ALU.subtract).then_inc(sem("scan_r"), 1)

            def post_c(step):
                d = step[0]
                D = d_full(step, "kv")
                dve.wait_ge(sem("scan_sg"), now(step))
                v.tensor_tensor(S[d], S[d], heads(D[:]), ALU.add).then_inc(sem(f"scan_dread{d}"), 1)

            def turn(own, post, pre):
                own_lat = own and own[1]
                for lv in range(1, LV):
                    if own:
                        level_a(own, lv)
                    if lv == 2 and own_lat:
                        g8(own, 1)
                    if lv == 3 and own_lat:
                        scores(own)
                    if lv == 4 and own_lat:
                        from_state(own)
                    if lv == 5 and own_lat:
                        from_chunk(own)
                    if lv == 6 and own:
                        to_state(own)
                    if lv == 6 and pre:
                        pre_c(pre)
                    if own:
                        level_b(own, lv)
                    if lv == 1 and post:
                        post_a(post)
                    if lv == 3 and post:
                        post_c(post)
                    if lv == 4 and pre:
                        pre_a(pre)
                    if lv == 5 and pre:
                        pre_b(pre)
                    if lv == 6 and pre:
                        pre_d(pre)

            turns(dve, turn)

        def pool_scan(pool):
            p = nc.gpsimd

            def turn(own, post, pre):
                if post:
                    d = post[0]
                    pool.wait_ge(sem("scan_ks"), now(post))
                    if post[1]:
                        pool.wait_ge(sem("scan_o"), now_lat(post))
                    p.tensor_tensor(S[d], S[d], bc(gs[d][:, Q_EGT, DN], P), ALU.mult).then_inc(sem("scan_sg"), 1)
                if pre:
                    d, lat, t = pre
                    ti = tile_of(lat, t, d)
                    if post:
                        pool.wait_ge(sem(f"scan_dread{d}"), d_before(post, "kv"))
                        pool.wait_ge(sem("scan_sg"), now(post))
                    p.tensor_copy(gs[d].rearrange("p q g -> p (q g)"),
                                  pack[:, bass.ds(ti, 1), d, :, :].rearrange("p a q g -> p (a q g)"))\
                        .then_inc(sem("scan_gs"), 1)
                    p.tensor_copy(kTs[d], kT[:, :, bass.ds(ti * P, P)]).then_inc(sem("scan_kst"), 1)
                    if lat:
                        p.tensor_copy(BTs[d], BT[:, :, bass.ds(ti * P, P)])
                        p.tensor_copy(CTs[d], CT[:, :, bass.ds(ti * P, P)])
                    p.tensor_copy(flat(Bts[d]), Btok[:, bass.ds(ti, 1), :].rearrange("p a n -> p (a n)"))\
                        .then_inc(sem("scan_cst"), 1)
                if own:
                    d, lat, t = own
                    if lat:
                        pool.wait_ge(sem(f"scan_dps{d}"), d_before(own, "yoff") + 1)
                    elif t == 0 and d == 0:
                        pool.wait_ge(sem("state0"), 4)
                    p.tensor_tensor(hs[d], hs[d], bc(gs[d][:, Q_EGT, SM], SSM_P), ALU.mult).then_inc(sem("scan_hg"), 1)
                if pre:
                    d, lat, t = pre
                    pool.wait_ge(sem("scan_gs"), now(pre))
                    pool.wait_ge(sem("scan_eexp"), now(pre))
                    p.tensor_tensor(E[d], E[d], bc(gs[d][:, Q_W, DN], P), ALU.mult).then_inc(sem("scan_ebeta"), 1)
                    xt = xtok[:, bass.ds(tile_of(lat, t, d), 1), :].rearrange("p a (h n) -> p (a h) n", h=SSM_H)
                    p.tensor_tensor(xdt[d], xt, bc(gs[d][:, Q_W, SM], SSM_P), ALU.mult)
                    p.tensor_tensor(xw[d], xt, bc(gs[d][:, Q_WT, SM], SSM_P), ALU.mult).then_inc(sem("scan_xst"), 1)
                    pool.wait_ge(sem("scan_egrow"), now(pre))
                    if lat:
                        p.tensor_tensor(qgT[d], qT[:, :, bass.ds(tile_of(lat, t, d) * P, P)], kgT[d], ALU.mult)\
                            .then_inc(sem("scan_qg"), 1)
                    pool.wait_ge(sem("scan_kst"), now(pre))
                    p.tensor_tensor(kgT[d], kTs[d], kgT[d], ALU.mult).then_inc(sem("scan_kg"), 1)

            pool.wait_ge(sem("pack"), 2)
            pool.wait_ge(sem("zps"), 2 * NL)
            for i in range(2):
                pool.wait_ge(sem(f"z_out{i}"), 16 * NL)
            p.memset(zero, 0.0).then_inc(sem("zero"), 1)
            turns(pool, turn)

        def sp_scan(sp_):
            for d in range(2):
                sp_.sem_inc(sem(f"ost_out{d}"), 16)
            y_zero_t = y_dram.rearrange("(t p) d -> t p d", p=P)
            sp_.wait_ge(sem("zero"), 1)
            for t in range(NL):
                for h in range(2):
                    sp_.dma_start(y_zero_t[t, :, h * 512:(h + 1) * 512], zero).then_inc(sem("y_zero"), 16)
            with sp_.Fori(0, NL - 1) as t:
                for d in range(2):
                    scan_store(sp_, d, t)

        def scan_store(sp_, d, t):
            sp_.wait_ge(sem("scan_oc"), t * 2 + (d + 3))
            sp_.wait_ge(sem(f"scan_dread{d}"), d_before((d, True, t), "ydiag") + 1)
            sp_.dma_start(scan_dram[d, bass.ds(tile_of(True, t, d), 1), :, :].rearrange("a p n -> (a p) n"),
                          ost[d]).then_inc(sem(f"ost_out{d}"), 16)

        at[0] = 0
        fb = [take(D) for _ in range(2)]
        bb = [take(D) for _ in range(2)]
        zb_ = [take(D) for _ in range(2)]
        xr = [take(D) for _ in range(2)]
        mixT = [take(D).rearrange("p (k n) -> p k n", k=KD) for _ in range(2)]
        h2 = [take(D) for _ in range(2)]
        h2T = [take(D).rearrange("p (k n) -> p k n", k=KD) for _ in range(2)]
        rowv = take(3 * D).rearrange("p (r n) -> p r n", r=3)
        assert at[0] <= XT0
        at[0] = W0
        wo = take(KD * D).rearrange("p (k n) -> p k n", k=KD)
        x2 = take(NL * D).rearrange("p (t n) -> p t n", t=NL)
        affT = take(T)[0:E_N, :]
        row5 = take(D)
        aff = take(NL * E_N).rearrange("p (t n) -> p t n", t=NL)
        sqj = take(D)
        tk = take(3 * P)
        topv, topf = tk[0:E_N, 0:CAP], tk[0:E_N, CAP:2 * CAP]
        topi = take(P).bitcast(U32)[0:E_N, 0:CAP]
        idxT = take(E_N).bitcast(U32)
        gateT = take(E_N)
        rcol = take(4 * KD).rearrange("p (r k) -> p r k", r=4)
        sq, rs, sm = ([take(8) for _ in range(2)] for _ in range(3))
        lmax = take(NL)
        at[0] = 0
        ew = []
        for _ in range(2):
            wg = take(KD * F).rearrange("p (k n) -> p k n", k=KD)
            wu = take(KD * F).rearrange("p (k n) -> p k n", k=KD)
            wd = take(KF * D).rearrange("p (k n) -> p k n", k=KF)
            ew.append((wg, wu, wd))
        NX = 4
        xs = [take(D) for _ in range(NX)]
        xsT = [take(D).rearrange("p (k n) -> p k n", k=KD) for _ in range(2)]
        hid = [take(F) for _ in range(2)]
        hidT = [take(F).rearrange("p (k n) -> p k n", k=KF) for _ in range(2)]
        ye = [take(D) for _ in range(2)]
        assert at[0] <= W0 + KD * D
        yt = arena[:, 0:NL * D].rearrange("p (t n) -> p t n", t=NL)

        wo_k = w_out.rearrange("a (k p) n -> (a p) k n", p=P)
        wg_e = exp_w_gate.rearrange("a e (k p) n -> (a e) p k n", p=P)
        wu_e = exp_w_up.rearrange("a e (k p) n -> (a e) p k n", p=P)
        wd_e = exp_w_down.rearrange("a e (k p) n -> (a e) p k n", p=P)
        h2_t = h2_dram.rearrange("(t p) d -> t p d", p=P)
        y_t = y_dram.rearrange("(t p) d -> t p d", p=P)
        out_t = out.rearrange("a (t p) d -> (a t) p d", p=P)
        N_SCAN = NC * len(D_CTX) + NL * len(D_LAT)

        ORD = [NL // 2 - 1 - t // 2 if t % 2 == 0 else NL // 2 + t // 2 for t in range(NL)]

        def scan_over(eng):
            eng.wait_ge(sem("y_zero"), 32 * NL)
            for d in range(2):
                eng.wait_ge(sem(f"scan_dread{d}"), N_SCAN)
                eng.wait_ge(sem("scan_oc"), 2 * (NL + 1))
                eng.wait_ge(sem(f"ost_out{d}"), 16 * (NL + 1))

        def sp_tail(sp_):
            sp_.wait_ge(sem("scan_kst"), 2 * NT)
            sp_.wait_ge(sem("scan_qg"), 2 * NL)
            for d in range(2):
                sp_.wait_ge(sem(f"scan_dps{d}"), d_before((d, True, NL - 1), "sqk") + 1)
                sp_.wait_ge(sem(f"ost_out{d}"), 16 * (NL // 2 + 2))

            def load(t):
                s = t % 2
                o = ORD[t]
                if t >= 2:
                    sp_.wait_ge(sem("fbT"), t - 1)
                for dst, src in ((fb[s], scan_dram[0, o]), (bb[s], scan_dram[1, o]), (zb_[s], z_dram[o])):
                    sp_.dma_start(dst, src).then_inc(sem(f"m_in{s}"), 16)
                if t >= 2:
                    sp_.wait_ge(sem("x2"), t - 1)
                sp_.dma_start(xr[s], x_t[o]).then_inc(sem(f"xr_in{s}"), 16)
            load(0)
            load(1)
            for d in range(2):
                scan_store(sp_, d, NL - 1)
            scan_over(sp_)
            for h in range(2):
                sp_.dma_start(wo[:, :, h * 512:(h + 1) * 512], wo_k[:, :, h * 512:(h + 1) * 512])\
                    .then_inc(sem(f"wo_in{h}"), 16)
            for t in range(2, NL):
                load(t)
            sp_.wait_ge(sem("h2ps"), NL)
            sp_.wait_ge(sem("mps"), NL)
            for i in range(2):
                sp_.wait_ge(sem(f"h2_out{i}"), 16 * NL // 2)

            def load_expert(e, s):
                sp_.dma_start(ew[s][0], wg_e[e]).then_inc(sem(f"gu_in{s}"), 16)
                sp_.dma_start(ew[s][1], wu_e[e]).then_inc(sem(f"gu_in{s}"), 16)
                sp_.dma_start(ew[s][2], wd_e[e]).then_inc(sem(f"d_in{s}"), 16)
            for e in range(E_N):
                if e == 1:
                    sp_.wait_ge(sem("logit"), NL)
                    sp_.wait_ge(sem("y_zero"), 32 * NL)
                if e >= 2:
                    sp_.wait_ge(sem("down"), e - 1)
                load_expert(e, e % 2)
            sp_.wait_ge(sem("y_sc"), 16 * E_N)
            sp_.wait_ge(sem("down"), E_N)
            for t in range(NL):
                sp_.dma_start(yt[:, t, :], y_t[t]).then_inc(sem(f"tile_in{t // 2}"), 16)
            for t in range(NL):
                sp_.wait_ge(sem("fin"), t + 1)
                sp_.dma_start(out_t[t], yt[:, t, :]).then_inc(sem("out"), 16)
            sp_.wait_ge(sem("out"), 16 * NL)

        def pe_tail(pe):
            mm, tr = nc.tensor.matmul, nc.tensor.transpose
            scan_over(pe)
            for r in range(4):
                if r >= 2:
                    pe.wait_ge(sem("rowv"), r - 1)
                elif r == 0:
                    pe.wait_ge(sem("rcol"), 1)
                for k in range(KD):
                    last = tr(ps[2 * (r % 2) + k // 4][:, (k % 4) * P:(k % 4 + 1) * P], rcol[:, r, k:k + 1].to_broadcast([P, P]),
                              ident[:])
                last.then_inc(sem("rowps"), 1)
            pe.wait_ge(sem("rowv"), 4)

            def back(t):
                s = t % 2
                pe.wait_ge(sem("h2"), t + 1)
                if t >= 1:
                    pe.wait_ge(sem("h2T"), t)
                for k in range(KD):
                    last = tr(ps[6 + k // 4][:, (k % 4) * P:(k % 4 + 1) * P], h2[s][:, k * P:(k + 1) * P], ident[:])
                last.then_inc(sem("h2ps"), 1)

            def router(t):
                s = t % 2
                pe.wait_ge(sem("h2T"), t + 1)
                if t >= 1:
                    pe.wait_ge(sem("lcopy"), t)
                for k in range(KD):
                    last = mm(ps[1][:, 0:E_N], h2T[s][:, k, :], rw[:, k, :], start=(k == 0), stop=(k == KD - 1))
                last.then_inc(sem("logit"), 1)

            for t in range(NL):
                s = t % 2
                pe.wait_ge(sem("mixed"), t + 1)
                if t >= 3:
                    pe.wait_ge(sem("lcopy"), t - 2)
                for k in range(KD):
                    last = tr(ps[k // 4][:, (k % 4) * P:(k % 4 + 1) * P], fb[s][:, k * P:(k + 1) * P], ident[:])
                last.then_inc(sem("fbT"), 1)
                if t >= 2:
                    back(t - 2)
                pe.wait_ge(sem("mixT"), t + 1)
                if t >= 2:
                    pe.wait_ge(sem("x2"), t - 1)
                for h in range(2):
                    if t == 0:
                        pe.wait_ge(sem(f"wo_in{h}"), 16)
                    for k in range(KD):
                        last = mm(ps[2 + 2 * s + h][:], mixT[s][:, k, :], wo[:, k, h * 512:(h + 1) * 512],
                                  start=(k == 0), stop=(k == KD - 1))
                    if h == 0 and t >= 2:
                        router(t - 2)
                last.then_inc(sem("mps"), 1)
            for t in range(NL - 2, NL):
                back(t)
                router(t)
            pe.wait_ge(sem("aff"), 1)
            for t in range(NL):
                last = tr(ps[2 + t // 4][0:E_N, (t % 4) * P:(t % 4 + 1) * P], aff[:, t, :], ident[:])
            last.then_inc(sem("affps"), 1)
            pe.wait_ge(sem("topk"), 2)
            tr(ps[0][:, 0:E_N], topf, ident[0:E_N, 0:E_N])
            tr(ps[0][:, E_N:2 * E_N], topv, ident[0:E_N, 0:E_N]).then_inc(sem("topT"), 1)
            pe.wait_ge(sem("idx"), 2)

            def xs_transposed(e):
                pe.wait_ge(sem(f"xs_in{e % NX}"), 16 * (e // NX + 1))
                if e >= 1:
                    pe.wait_ge(sem("xsT"), e)
                for k in range(KD):
                    last = tr(ps[k // 4][:, (k % 4) * P:(k % 4 + 1) * P], xs[e % NX][:, k * P:(k + 1) * P], ident[:])
                last.then_inc(sem("xsps"), 1)

            xs_transposed(0)
            for e in range(E_N):
                s = e % 2
                pe.wait_ge(sem("xsT"), e + 1)
                pe.wait_ge(sem(f"gu_in{s}"), 32 * (e // 2 + 1))
                if e >= 1:
                    pe.wait_ge(sem("hidT"), e)
                for j in range(2):
                    for k in range(KD):
                        last = mm(ps[2 + j][:], xsT[s][:, k, :], ew[s][j][:, k, :], start=(k == 0), stop=(k == KD - 1))
                last.then_inc(sem("gu"), 1)
                if e + 1 < E_N:
                    xs_transposed(e + 1)
                pe.wait_ge(sem("hid"), e + 1)
                for k in range(KF):
                    last = tr(ps[4][:, k * P:(k + 1) * P], hid[s][:, k * P:(k + 1) * P], ident[:])
                last.then_inc(sem("hidps"), 1)
                pe.wait_ge(sem("hidT"), e + 1)
                pe.wait_ge(sem(f"d_in{s}"), 16 * (e // 2 + 1))
                if e >= 1:
                    pe.wait_ge(sem("ye"), e)
                for h in range(2):
                    for k in range(KF):
                        last = mm(ps[5 + h][:], hidT[s][:, k, :], ew[s][2][:, k, h * 512:(h + 1) * 512],
                                  start=(k == 0), stop=(k == KF - 1))
                last.then_inc(sem("down"), 1)

        def act_tail(act):
            a = nc.scalar.activation
            scan_over(act)

            def sqrt_of(src, dst, n, name, c):
                a(dst, src, ACT.Sqrt, scale=1.0 / n, bias=eps1[:]).then_inc(sem(name), c)

            def front(t):
                s = t % 2
                act.wait_ge(sem("merged"), t + 1)
                for h in range(DN_H):
                    a(sqj[:, h * P:(h + 1) * P], fb[s][:, h * P:(h + 1) * P], ACT.Square, accum_out=sq[s][:, h:h + 1])
                for g in range(SSM_G):
                    last = a(sqj[:, QK + g * 256:QK + (g + 1) * 256], fb[s][:, QK + g * 256:QK + (g + 1) * 256],
                             ACT.Square, accum_out=sq[s][:, DN_H + g:DN_H + g + 1])
                last.then_inc(sem("fsq"), 1)
                act.wait_ge(sem("fsq"), t + 1)
                a(rs[s][:, 0:DN_H], sq[s][:, 0:DN_H], ACT.Sqrt, scale=1.0 / P, bias=eps1[:])
                sqrt_of(sq[s][:, DN_H:DN_H + SSM_G], rs[s][:, DN_H:DN_H + SSM_G], DI // SSM_G, "fsqrt", 1)

            def mix_t(t):
                s = t % 2
                act.wait_ge(sem("fbT"), t + 1)
                if t >= 2:
                    act.wait_ge(sem("mps"), t - 1)
                a(mixT[s][:, 0:DN_H, :], heads(ps[0][:]), ACT.Copy, scale=vcols[:, V_DG:V_DG + 1])
                for k in range(4):
                    last = a(mixT[s][:, 4 + k, :], ps[1][:, k * P:(k + 1) * P], ACT.Copy,
                             scale=vcols[:, V_SG + k:V_SG + k + 1])
                last.then_inc(sem("mixT"), 1)

            def back_sum(t):
                s = t % 2
                act.wait_ge(sem("mps"), t + 1)
                if t >= 1:
                    act.wait_ge(sem("bsq"), 4 * t)
                for h in range(2):
                    a(sqj[:, h * 512:(h + 1) * 512], ps[2 + 2 * s + h][:], ACT.Square, accum_out=sm[s][:, h:h + 1])\
                        .then_inc(sem("bsq"), 1)
                act.wait_ge(sem("msum"), t + 1)
                a(sm[s][:, 2:3], sm[s][:, 2:3], ACT.Sqrt, scale=1.0 / D, bias=eps1[:]).then_inc(sem("bsqrt"), 1)

            def back_x2(t):
                s = t % 2
                act.wait_ge(sem("x2"), t + 1)
                a(sqj[:, 0:D], x2[:, ORD[t], :], ACT.Square, accum_out=sm[s][:, 3:4]).then_inc(sem("bsq"), 1)
                act.wait_ge(sem("bsq"), 4 * t + 3)
                a(sm[s][:, 3:4], sm[s][:, 3:4], ACT.Sqrt, scale=1.0 / D, bias=eps1[:]).then_inc(sem("bsq"), 1)

            def h2_t(t):
                s = t % 2
                act.wait_ge(sem("h2ps"), t + 1)
                if t >= 2:
                    act.wait_ge(sem("logit"), t - 1)
                for h in range(2):
                    last = a(h2T[s][:, 4 * h:4 * h + 4, :], heads(ps[6 + h][:]), ACT.Copy)
                last.then_inc(sem("h2T"), 1)

            front(0)
            for t in range(NL + 2):
                if t < NL:
                    mix_t(t)
                if t >= 2:
                    h2_t(t - 2)
                if t + 1 < NL:
                    front(t + 1)
                if 1 <= t <= NL:
                    back_sum(t - 1)
                    back_x2(t - 1)
            act.wait_ge(sem("lmax"), 1)
            a(aff, aff, ACT.Exp).then_inc(sem("lexp"), 1)
            act.wait_ge(sem("affps"), 1)
            for h in range(2):
                a(affT[:, h * 512:(h + 1) * 512], ps[2 + h][0:E_N, :], ACT.Copy).then_inc(sem("affT"), 1)
            for e in range(E_N + 1):
                if e < E_N:
                    s = e % 2
                    act.wait_ge(sem("xsps"), e + 1)
                    if e >= 2:
                        act.wait_ge(sem("gu"), e - 1)
                    for h in range(2):
                        last = a(xsT[s][:, 4 * h:4 * h + 4, :], heads(ps[h][:]), ACT.Copy)
                    last.then_inc(sem("xsT"), 1)
                if e >= 1:
                    s = (e - 1) % 2
                    act.wait_ge(sem("hidps"), e)
                    a(hidT[s], heads(ps[4][:]), ACT.Copy).then_inc(sem("hidT"), 1)
                if e < E_N:
                    s = e % 2
                    act.wait_ge(sem("gu"), e + 1)
                    a(hid[s], ps[2][:], ACT.Silu).then_inc(sem("sg"), 1)
            for t in range(NL):
                act.wait_ge(sem(f"tile_in{t // 2}"), 64)
                a(x2dead, yt[:, t, :], ACT.Square, accum_out=ssq[:, t:t + 1]).then_inc(sem("ysq"), 1)
                act.wait_ge(sem("ysq"), 2 * t + 1)
                a(rstd[:, t:t + 1], ssq[:, t:t + 1], ACT.Sqrt, scale=1.0 / D, bias=eps1[:]).then_inc(sem("ysq"), 1)
        x2dead = sqj

        def dve_tail(dve, link):
            v = nc.vector
            scan_over(dve)
            m = mods[:, :, 0]
            g = vcols[:, V_NG:V_CB].rearrange("p (r k) -> p r k", k=KD)
            link(v.tensor_tensor(m[:, 2 * KD:6 * KD], m[:, 2 * KD:6 * KD], vcols[:, V_AB + 2 * KD:V_NG], ALU.add))
            v.tensor_tensor(rcol[:, 0, :], m[:, 2 * KD:3 * KD], g[:, 1, :], ALU.mult)
            v.scalar_tensor_tensor(rcol[:, 1, :], m[:, 4 * KD:5 * KD], 1.0, g[:, 2, :], ALU.add, ALU.mult)
            v.tensor_copy(rcol[:, 2, :], m[:, 3 * KD:4 * KD])
            v.tensor_tensor(rcol[:, 3, :], m[:, 5 * KD:6 * KD], g[:, 3, :], ALU.mult).then_inc(sem("rcol"), 1)
            def front(t):
                s = t % 2
                dve.wait_ge(sem(f"m_in{s}"), 48 * (t // 2 + 1))
                link(v.tensor_tensor(fb[s], fb[s], bb[s], ALU.add))
                link(v.tensor_tensor(heads(bb[s][:, QK:D], SSM_H),
                                     xtok[:, ORD[t], :].rearrange("p (h n) -> p h n", h=SSM_H),
                                     bc(sbc[:, 48:56], SSM_P), ALU.mult))
                link(v.tensor_tensor(fb[s][:, QK:D], fb[s][:, QK:D], bb[s][:, QK:D], ALU.add))
                v.tensor_tensor(fb[s][:, QK:D], fb[s][:, QK:D], zb_[s][:, QK:D], ALU.mult).then_inc(sem("merged"), 1)

            def front_r(t):
                s = t % 2
                dve.wait_ge(sem("fsqrt"), t + 1)
                link(v.reciprocal(rs[s][:, 0:6], rs[s][:, 0:6]))
                link(v.tensor_tensor(heads(fb[s][:, 0:QK]), heads(fb[s][:, 0:QK]), bc(rs[s][:, 0:DN_H], P), ALU.mult))
                v.tensor_tensor(fb[s][:, 0:QK], fb[s][:, 0:QK], zb_[s][:, 0:QK], ALU.mult)
                v.tensor_tensor(heads(fb[s][:, QK:D], SSM_G), heads(fb[s][:, QK:D], SSM_G),
                                bc(rs[s][:, DN_H:6], 256), ALU.mult).then_inc(sem("mixed"), 1)

            def back_sum(t):
                s = t % 2
                dve.wait_ge(sem("bsq"), 4 * t + 2)
                v.tensor_tensor(sm[s][:, 2:3], sm[s][:, 0:1], sm[s][:, 1:2], ALU.add).then_inc(sem("msum"), 1)

            def back_x2(t):
                s = t % 2
                dve.wait_ge(sem("bsqrt"), t + 1)
                link(v.reciprocal(sm[s][:, 2:3], sm[s][:, 2:3]))
                for h in range(2):
                    hs_ = slice(h * 512, (h + 1) * 512)
                    ins = v.scalar_tensor_tensor(x2[:, ORD[t], hs_], ps[2 + 2 * s + h][:], sm[s][:, 2:3], rowv[:, 0, hs_],
                                                 ALU.mult, ALU.mult)
                link(ins)
                dve.wait_ge(sem(f"xr_in{s}"), 16 * (t // 2 + 1))
                v.tensor_tensor(x2[:, ORD[t], :], x2[:, ORD[t], :], xr[s], ALU.add).then_inc(sem("x2"), 1)

            def back_h2(t):
                s = t % 2
                dve.wait_ge(sem("bsq"), 4 * t + 4)
                link(v.reciprocal(sm[s][:, 3:4], sm[s][:, 3:4]))
                if t >= 2:
                    dve.wait_ge(sem(f"h2_out{s}"), 16 * (t // 2))
                    dve.wait_ge(sem("h2ps"), t - 1)
                link(v.scalar_tensor_tensor(h2[s], x2[:, ORD[t], :], sm[s][:, 3:4], rowv[:, 1, :], ALU.mult, ALU.mult))
                v.tensor_tensor(h2[s], h2[s], rowv[:, 2, :], ALU.add).then_inc(sem("h2"), 1)

            front(0)
            for r in range(4):
                dve.wait_ge(sem("rowps"), r + 1)
                dst = rowv[:, r, :] if r < 3 else row5
                v.tensor_copy(dst[:, 0:512], ps[2 * (r % 2)][:])
                v.tensor_copy(dst[:, 512:D], ps[2 * (r % 2) + 1][:]).then_inc(sem("rowv"), 1)
            for t in range(NL + 2):
                if t < NL:
                    front_r(t)
                if t + 1 < NL:
                    front(t + 1)
                if 1 <= t <= NL:
                    back_sum(t - 1)
                    back_x2(t - 1)
                    back_h2(t - 1)
                if t >= 2:
                    dve.wait_ge(sem("logit"), t - 1)
                    v.tensor_copy(aff[:, ORD[t - 2], :], ps[1][:, 0:E_N]).then_inc(sem("lcopy"), 1)
            dve.wait_ge(sem("lcopy"), NL)
            link(v.reduce_max(lmax, aff, AX.X))
            v.tensor_tensor(aff, aff, bc(lmax, E_N), ALU.subtract).then_inc(sem("lmax"), 1)
            dve.wait_ge(sem("lexp"), 1)
            link(v.reduce_sum(lmax, aff, AX.X))
            link(v.reciprocal(lmax, lmax))
            v.tensor_tensor(aff, aff, bc(lmax, E_N), ALU.mult).then_inc(sem("aff"), 1)
            dve.wait_ge(sem("affT"), 2)
            for r in range(CAP // 8):
                c = slice(8 * r, 8 * r + 8)
                link(v.max(topv[:, c], affT))
                link(v.max_index(topi[:, c], topv[:, c], affT))
                if r < CAP // 8 - 1:
                    link(v.match_replace(affT, topv[:, c], affT, -1.0))
            v.tensor_copy(topf, topi).then_inc(sem("topk"), 2)
            dve.wait_ge(sem("topT"), 1)
            v.tensor_copy(idxT, ps[0][:, 0:E_N]).then_inc(sem("idx"), 1)
            v.tensor_copy(gateT, ps[0][:, E_N:2 * E_N]).then_inc(sem("idx"), 1)
            dve.wait_ge(sem("idx"), 2)
            for e in range(E_N):
                s = e % 2
                dve.wait_ge(sem("sg"), e + 1)
                v.tensor_tensor(hid[s], hid[s], ps[3][:], ALU.mult).then_inc(sem("hid"), 1)
                dve.wait_ge(sem("down"), e + 1)
                if e >= 2:
                    dve.wait_ge(sem("y_sc"), 16 * (e - 1))
                v.tensor_scalar(ye[s][:, 0:512], ps[5][:], gateT[:, e:e + 1], None, ALU.mult)
                v.tensor_scalar(ye[s][:, 512:D], ps[6][:], gateT[:, e:e + 1], None, ALU.mult).then_inc(sem("ye"), 1)
            for t in range(NL):
                dve.wait_ge(sem("ysq"), 2 * t + 2)
                link(v.reciprocal(rstd[:, t:t + 1], rstd[:, t:t + 1]))
                link(v.scalar_tensor_tensor(yt[:, t, :], yt[:, t, :], rstd[:, t:t + 1], row5, ALU.mult, ALU.mult))
                v.tensor_tensor(yt[:, t, :], yt[:, t, :], x2[:, t, :], ALU.add).then_inc(sem("fin"), 1)

        def pool_tail(pool):
            p = nc.gpsimd
            scan_over(pool)
            for t in range(NL):
                pool.wait_ge(sem("h2"), t + 1)
                pool.dma_start(h2_t[ORD[t]], h2[t % 2]).then_inc(sem(f"h2_out{t % 2}"), 16)
            pool.wait_ge(sem("idx"), 2)
            for i in range(2):
                pool.wait_ge(sem(f"h2_out{i}"), 16 * NL // 2)
            pool.wait_ge(sem("y_zero"), 32 * NL)

            def gather(e):
                p.indirect_dma_start(xs[e % NX], None, h2_dram,
                                     bass.IndirectOffsetOnAxis(ap=idxT[:, e:e + 1], axis=0))\
                    .then_inc(sem(f"xs_in{e % NX}"), 16)
            for e in range(NX):
                gather(e)
            for e in range(E_N):
                if 1 <= e <= E_N - NX:
                    pool.wait_ge(sem("xsps"), e)
                    gather(e + NX - 1)
                pool.wait_ge(sem("ye"), e + 1)
                if e >= 1:
                    pool.wait_ge(sem("y_sc"), 16 * e)
                p.indirect_dma_start(y_dram, bass.IndirectOffsetOnAxis(ap=idxT[:, e:e + 1], axis=0), ye[e % 2], None,
                                     compute_op=ALU.add).then_inc(sem("y_sc"), 16)

        N_C1 = 10 + 2 * 7 * 3
        block = es.enter_context(nc.Block())

        small = [(vrows[V_C:V_CC, :], c.rearrange("a (j p) -> (a j) p", p=P)),
                 (vrows[V_CC:V_AB, :], c_ctx.rearrange("(j p) -> j p", p=P)),
                 (vrows[V_AB:V_NG, :], ada_b.rearrange("a (j p) -> (a j) p", p=P)),
                 (vrows[V_NG:V_CB, :], norm_g.rearrange("a b (j p) -> (a b j) p", p=P)),
                 (vrows[V_CB:V_DG, :], conv_b.rearrange("a (j p) -> (a j) p", p=P)),
                 (vrows[V_DG:V_SG, :], dn_norm_g),
                 (vrows[V_SG:NV, :], ssm_norm_g.rearrange("a (j p) -> (a j) p", p=P)),
                 (srow[0:1, 0:24].rearrange("o (d g) -> o d g", d=2)[:, :, 0:DN_H], dn_dt_bias),
                 (srow[0:1, 0:24].rearrange("o (d g) -> o d g", d=2)[:, :, DN_H:GD], ssm_dt_bias),
                 (srow[0:1, 24:48].rearrange("o (d g) -> o d g", d=2)[:, :, 0:DN_H], dn_A_log),
                 (srow[0:1, 24:48].rearrange("o (d g) -> o d g", d=2)[:, :, DN_H:GD], ssm_A_log),
                 (srow[0:1, 48:56], ssm_D)]

        def late_load(b):
            nc.sync.dma_start(lring[b % 2], ada_k[:, :, (NAB + b) * 512:(NAB + b + 1) * 512])\
                .then_inc(sem(f"late_in{b % 2}"), 16)

        @block.sync
        def _(sp_):
            for dst, src in small:
                sp_.dma_start(dst, src).then_inc(sem("small_in"), 16)
            for b in range(3):
                sp_.dma_start(aring[b], ada_k[:, :, b * 512:(b + 1) * 512])\
                    .then_inc(sem(f"ada_in{b % 3}"), 16)
            for b in range(3, NAB):
                sp_.wait_ge(sem("ada_used"), b - 2)
                sp_.dma_start(aring[b % 3], ada_k[:, :, b * 512:(b + 1) * 512])\
                    .then_inc(sem(f"ada_in{b % 3}"), 16)
            for t in range(NT):
                src = x_t[t] if t < NL else ctx_t[t - NL]
                sp_.dma_start(xall[:, t, :], src).then_inc(sem(f"tile_in{t // 2}"), 16)
            sp_.dma_start(wring[0][:, :, 0:NGATE], w_k[:, :, OFF_GATE:OFF_GATE + NGATE]).then_inc(sem("w_in0"), 16)
            for m in range(NM):
                s = (m + 1) % NW
                if m + 1 >= NW:
                    sp_.wait_ge(sem("w_used"), m + 1 - NW + 1)
                col = tiles[m][0]
                sp_.dma_start(wring[s], w_k[:, :, col:col + P]).then_inc(sem(f"w_in{s}"), 16)
                if NW - 1 <= m < NW + 1:
                    late_load(m - NW + 1)
                elif 2 <= m - NW - 1 < NLB:
                    b = m - NW - 1
                    sp_.wait_ge(sem("aux_used"), n_aux(b - 2 + LATE - 1) + 1)
                    late_load(b)
            for i in range(NM + 1, NM + 1 + NW):
                s = i % NW
                sp_.wait_ge(sem("w_used"), i - NW + 1)
                sp_.dma_start(wring[s], w_k[:, :, OFF_Z + s * P:OFF_Z + (s + 1) * P]).then_inc(sem(f"w_in{s}"), 16)
            sp_.wait_ge(sem("conv"), NM)
            sp_.wait_ge(sem("silu"), NM)
            sp_.dma_start(wz1, w_k[:, :, OFF_Z + 512:OFF_Z + 1024]).then_inc(sem("wz_in"), 16)
            sp_scan(sp_)
            sp_tail(sp_)

        def arrived(eng, m):
            s = (m + 1) % NW
            eng.wait_ge(sem(f"w_in{s}"), 16 * ((m + 1) // NW + 1))

        @block.gpsimd
        def _(pool):
            nc.gpsimd.memset(ident[:], 0.0).then_inc(sem("c1"), 1)
            nc.gpsimd.memset(ones[:], 1.0).then_inc(sem("c1"), 1)
            nc.gpsimd.memset(neg_mask[:], 0.0).then_inc(sem("c1"), 1)
            nc.gpsimd.memset(cum_mask[:], 1.0).then_inc(sem("c1"), 1)
            nc.gpsimd.memset(lvl_mask[:], 1.0).then_inc(sem("c1"), 1)
            pool.wait_ge(sem("c1"), 5)
            nc.gpsimd.affine_select(out=ident[:], in_=ident[:], compare_op=ALU.not_equal, fill=1.0,
                                    base=0, pattern=[[-1, P]], channel_multiplier=1).then_inc(sem("c1"), 1)
            for d, s in ((0, 1), (1, -1)):
                nc.gpsimd.affine_select(out=neg_mask[:, d, :], in_=neg_mask[:, d, :], compare_op=ALU.is_ge,
                                        fill=NEG, base=0, pattern=[[s, P]], channel_multiplier=-s)\
                    .then_inc(sem("c1"), 1)
                nc.gpsimd.affine_select(out=cum_mask[:, d, :], in_=cum_mask[:, d, :], compare_op=ALU.is_ge,
                                        fill=0.0, base=0, pattern=[[s, P]], channel_multiplier=-s)\
                    .then_inc(sem("c1"), 1)
            n = 10
            for d in range(2):
                for lv in range(7):
                    s = 1 << lv
                    m = lvl_mask[:, d, lv, :].rearrange("p (b s) -> p b s", s=2 * s)
                    nb = P // (2 * s)
                    un = m[:, :, s:2 * s] if d == 0 else m[:, :, 0:s]
                    us = m[:, :, 0:s] if d == 0 else m[:, :, s:2 * s]
                    nc.gpsimd.memset(un, 0.0).then_inc(sem("c1"), 1)
                    n += 1
                    lo = s if d == 0 else 0
                    nc.gpsimd.affine_select(out=us, in_=us, compare_op=ALU.is_ge, fill=0.0, base=-lo,
                                            pattern=[[-2 * s, nb], [0, s]], channel_multiplier=1)\
                        .then_inc(sem("c1"), 1)
                    n += 1
                    pool.wait_ge(sem("c1"), n)
                    nc.gpsimd.affine_select(out=us, in_=us, compare_op=ALU.is_ge, fill=0.0, base=lo + s - 1,
                                            pattern=[[2 * s, nb], [0, s]], channel_multiplier=-1)\
                        .then_inc(sem("c1"), 1)
                    n += 1
            assert n == N_C1
            for m in range(NM):
                kind, i, has_ctx = tiles[m][1:]
                if kind in "kq":
                    n_kq = i + 1 if kind == "k" else DN_H + i + 1
                    dst = {"k": kT, "q": qT}[kind][:, i, :]
                    pool.wait_ge(sem("nrm_rec"), n_kq)
                    nc.gpsimd.tensor_tensor(dst, dst, ctmp[:, 0:TA if has_ctx else T], ALU.mult)\
                        .then_inc(sem("nrm_mul"), 1)
            pool_scan(pool)
            pool_tail(pool)

        zbank = (ps[0], ps[1], ps[2], ps[6])
        XG = [(0, 4), (4, 4), (8, 2)]
        assert NL == 8 and NC == 2

        def parts_of(m):
            return [(0, 512), (512, 512)] + ([(1024, TC)] if tiles[m][3] else [])

        def n_kq(m):
            return sum(tl[1] in "kq" for tl in tiles[:m])

        @block.tensor
        def _(pe):
            pe.wait_ge(sem("c1"), 6)
            pe.wait_ge(sem("small_in"), 16 * len(small))
            nc.tensor.transpose(ps[0][:, 0:NV], vrows, ident[0:NV, 0:NV]).then_inc(sem("vT"), 1)
            nc.tensor.matmul(ps[1][:, 0:56], ones[0:1, :], srow[0:1, :], start=True, stop=True)\
                .then_inc(sem("vT"), 1)
            pe.wait_ge(sem("silu_c"), 2)
            for b in range(NAB):
                pe.wait_ge(sem(f"ada_in{b % 3}"), 16 * (b // 3 + 1))
                if b >= 2:
                    pe.wait_ge(sem("mrow"), b - 1)
                for k in range(KD):
                    last = nc.tensor.matmul(ps[2 + b % 2][0:2, :], silu_c[:, k, :], aring[b % 3][:, k, :],
                                            start=(k == 0), stop=(k == KD - 1))
                last.then_inc(sem("ada_used"), 1)
            pe.wait_ge(sem("mrow"), NAB)
            pe.wait_ge(sem("vcols"), 2)
            for j in range(2 * KD):
                last = nc.tensor.transpose(ps[1][:, 2 * j:2 * j + 2], mrow[:, j * P:(j + 1) * P], ident[0:2, 0:2])
            last.then_inc(sem("vT"), 1)
            n = 0
            for t0, nt in XG:
                pe.wait_ge(sem("xn"), t0 + nt)
                for k in range(KD):
                    if n >= 4:
                        pe.wait_ge(sem("hT"), n - 3)
                    for i in range(nt):
                        last = nc.tensor.transpose(ps[4 + n % 4][:, i * P:(i + 1) * P],
                                                   xall[:, t0 + i, k * P:(k + 1) * P], ident[:])
                    last.then_inc(sem("xT"), 1)
                    n += 1
            pe.wait_ge(sem("hT"), n)
            pe.wait_ge(sem("w_in0"), 16)
            for gi, (o, w) in enumerate(parts_of(0)):
                for k in range(KD):
                    last = nc.tensor.matmul(ps[3 + gi][0:NGATE, 0:w], wring[0][:, k, 0:NGATE], hT[:, k, o:o + w],
                                            start=(k == 0), stop=(k == KD - 1))
            last.then_inc(sem("w_used"), 1)
            pe.wait_ge(sem("graw"), 1)
            for t in range(NT):
                last = nc.tensor.transpose(ps[7][:, t * NGATE:(t + 1) * NGATE], ctmp[0:NGATE, t * P:(t + 1) * P],
                                           ident[0:NGATE, 0:NGATE])
            last.then_inc(sem("Gps"), 1)
            aux = 0
            for m in range(NM + 1):
                if m < NM:
                    arrived(pe, m)
                    if m >= 2:
                        pe.wait_ge(sem("cin"), m - 1)
                    if m == 1:
                        pe.wait_ge(sem("graw"), 1)
                    for gi, (o, w) in enumerate(parts_of(m)):
                        for k in range(KD):
                            last = nc.tensor.matmul(ps[3 * (m % 2) + gi][:, 0:w], wring[(m + 1) % NW][:, k, :],
                                                    hT[:, k, o:o + w], start=(k == 0), stop=(k == KD - 1))
                    last.then_inc(sem("w_used"), 1)
                if m == 0:
                    pe.wait_ge(sem("logg"), 1)
                    pe.wait_ge(sem("c1"), N_C1)
                    for d in range(2):
                        nc.tensor.matmul(ps[7][:, d * NT * GD:(d + 1) * NT * GD], cum_mask[:, d, :],
                                         ga[:, :, d, :], start=True, stop=True)
                    nc.tensor.matmul(ps[7][:, 240:480], ones[:], ga[:].rearrange("p t d g -> p (t d g)"),
                                     start=True, stop=True).then_inc(sem("Gps"), 1)
                if late_before(m + 1) > late_before(m):
                    b = m - LATE
                    pe.wait_ge(sem("late"), b + 1)
                    pe.wait_ge(sem("aux_used"), aux - 1)
                    for q in range(4):
                        last = nc.tensor.matmul(ps[6 + aux % 2][:, q:q + 1], lring[b % 2][:, 0, q * P:(q + 1) * P],
                                                ones[:, 0:1], start=True, stop=True)
                    last.then_inc(sem("aux"), 1)
                    aux += 1
                if m >= 1:
                    kind, i, has_ctx = tiles[m - 1][1:]
                    if kind != "C":
                        pe.wait_ge(sem("silu"), m)
                    if m == 1:
                        pe.wait_ge(sem("Gev"), 2)
                    if kind in "kq":
                        for o, w in parts_of(m - 1):
                            if aux >= 2:
                                pe.wait_ge(sem("aux_used"), aux - 1)
                            nc.tensor.matmul(ps[6 + aux % 2][:, 0:w], ones[:], ctmp[:, o:o + w],
                                             start=True, stop=True).then_inc(sem("aux"), 1)
                            aux += 1
                    elif kind in "vxB":
                        src = BT[:, i, :] if kind == "B" else ctmp
                        for t0, nt in XG:
                            if aux >= 2:
                                pe.wait_ge(sem("aux_used"), aux - 1)
                            for q in range(nt):
                                last = nc.tensor.transpose(ps[6 + aux % 2][:, q * P:(q + 1) * P],
                                                           src[:, (t0 + q) * P:(t0 + q + 1) * P], ident[:])
                            last.then_inc(sem("aux"), 1)
                            aux += 1
            pe.wait_ge(sem("cin"), NM - 1)
            pe.wait_ge(sem("aux_used"), n_aux(NM))
            for zb in range(2 * NL):
                if zb == 0:
                    for i in range(NW):
                        arrived(pe, NM + i)
                if zb == NL:
                    pe.wait_ge(sem("wz_in"), 16)
                if zb >= 4:
                    pe.wait_ge(sem("zsb"), zb - 3)
                t = zb % NL
                for k in range(KD):
                    w = wz0[:, :, k, :] if zb < NL else wz1[:, k, :].rearrange("p (s n) -> p s n", s=NW)
                    last = nc.tensor.matmul(zbank[zb % 4][:].rearrange("p (s n) -> p s n", s=NW),
                                            hT[:, k, t * P:(t + 1) * P], w, start=(k == 0), stop=(k == KD - 1))
                last.then_inc(sem("zps"), 1)
            pe_scan(pe)
            pe_tail(pe)

        @block.scalar
        def _(act):
            act.dma_start(taps[:], taps_k).then_inc(sem("taps_in"), 16)
            act.dma_start(rw[:], rw_k).then_inc(sem("taps_in"), 16)
            act.wait_ge(sem("vcols"), 2)
            for j, v0 in enumerate((V_C, V_CC)):
                nc.scalar.activation(silu_c[:, :, j], vcols[:, v0:v0 + KD], ACT.Silu).then_inc(sem("silu_c"), 1)
            for t in range(NT):
                act.wait_ge(sem(f"tile_in{t // 2}"), 32)
                nc.scalar.activation(hflat[:, t * D:(t + 1) * D], xall[:, t, :], ACT.Square,
                                     accum_out=ssq[:, t:t + 1]).then_inc(sem("ssq"), 1)
                act.wait_ge(sem("ssq"), t + 1)
                nc.scalar.activation(rstd[:, t:t + 1], ssq[:, t:t + 1], ACT.Sqrt, scale=1.0 / D, bias=eps_d[:])\
                    .then_inc(sem("rms"), 1)
            act.wait_ge(sem("gain1"), 1)
            n = 0
            for t0, nt in XG:
                j = 0 if t0 < NL else 1
                for k in range(KD):
                    act.wait_ge(sem("xT"), n + 1)
                    nc.scalar.activation(hT[:, k, t0 * P:(t0 + nt) * P], ps[4 + n % 4][:, 0:nt * P], ACT.Identity,
                                         bias=mods[:, k, j:j + 1], scale=gain1[:, k, j:j + 1])\
                        .then_inc(sem("hT"), 1)
                    n += 1
            act.wait_ge(sem("w_used"), 1)
            for gi, (o, w) in enumerate(parts_of(0)):
                last = nc.scalar.activation(ctmp[0:NGATE, o:o + w], ps[3 + gi][0:NGATE, 0:w], ACT.Copy)
            last.then_inc(sem("graw"), 1)
            act.wait_ge(sem("gabs"), 2)
            nc.scalar.activation(beta_f, beta_f, ACT.Exp).then_inc(sem("gexp"), 1)
            nc.scalar.activation(gb[:], gb[:], ACT.Exp).then_inc(sem("gexp"), 1)
            nc.scalar.activation(gneg[:], sbc[:, 24:48].rearrange("p (d g) -> p d g", d=2), ACT.Exp)\
                .then_inc(sem("gexp"), 1)
            act.wait_ge(sem("gln"), 1)
            nc.scalar.activation(eG[:], G[:], ACT.Ln).then_inc(sem("gln_out"), 1)
            act.wait_ge(sem("Gev"), 3)
            nc.scalar.activation(eG[:], G[:], ACT.Exp).then_inc(sem("eG"), 1)
            nc.scalar.activation(eGt[:], gb[:], ACT.Exp).then_inc(sem("eG"), 1)
            nc.scalar.activation(wtail[:], ga[:], ACT.Exp).then_inc(sem("eG"), 1)

            aux = 0
            for m in range(NM + 1):
                if m >= 1:
                    mm = m - 1
                    col, kind, i, has_ctx = tiles[mm]
                    w = TA if has_ctx else T
                    act.wait_ge(sem("conv"), mm + 1)
                    if n_kq(mm):
                        act.wait_ge(sem("nrm_mul"), n_kq(mm))
                    dst = ctmp[:, 0:w] if kind in "vx" else {"k": kT, "q": qT, "B": BT, "C": CT}[kind][:, i, 0:w]
                    bcol = vcols[:, V_CB + col // P:V_CB + col // P + 1]
                    ins = nc.scalar.activation(dst, cacc[mm % 2][:, 0:w], ACT.Silu, bias=bcol)
                    if kind in "kq":
                        ins.then_inc(sem("silu_kq"), 1)
                        act.wait_ge(sem("silu_kq"), n_kq(mm) + 1)
                        ins = nc.scalar.activation(ctmp[:, 0:w], dst, ACT.Square)
                    ins.then_inc(sem("silu"), 1)
                if m < NM:
                    act.wait_ge(sem("w_used"), m + 2)
                    if m == 0:
                        act.wait_ge(sem("pad"), 4)
                    if m >= 2:
                        act.wait_ge(sem("conv"), m - 1)
                    for gi in range(2):
                        last = nc.scalar.activation(
                            cin_l[m % 2][:, 1 + 8 * gi:9 + 8 * gi, 1:1 + GW],
                            ps[3 * (m % 2) + gi][:].rearrange("p (r c) -> p r c", c=GW), ACT.Copy)
                    if tiles[m][3]:
                        last = nc.scalar.activation(cin_c[m % 2][:, 1:1 + TC], ps[3 * (m % 2) + 2][:, 0:TC],
                                                    ACT.Copy)
                    last.then_inc(sem("cin"), 1)
                if late_before(m + 1) > late_before(m):
                    act.wait_ge(sem("aux"), aux + 1)
                    j = 2 * KD + 4 * (m - LATE)
                    nc.scalar.activation(mods[:, j:j + 4, 0], ps[6 + aux % 2][:, 0:4], ACT.Copy)\
                        .then_inc(sem("aux_used"), 1)
                    aux += 1
                if m >= 1:
                    if kind in "kq":
                        f = 1.0 if kind == "k" else float(DK)
                        eb = eps1 if kind == "k" else eps_q
                        for o, ww in parts_of(mm):
                            act.wait_ge(sem("aux"), aux + 1)
                            nc.scalar.activation(ctmp[:, o:o + ww], ps[6 + aux % 2][:, 0:ww], ACT.Sqrt, scale=f,
                                                 bias=eb[:]).then_inc(sem("aux_used"), 1)
                            aux += 1
                    elif kind in "vxB":
                        for t0, nt in XG:
                            act.wait_ge(sem("aux"), aux + 1)
                            dstt = {"v": vtok, "x": xtok, "B": Btok}[kind]
                            nc.scalar.activation(dstt[:, t0:t0 + nt, i * P:(i + 1) * P],
                                                 ps[6 + aux % 2][:, 0:nt * P].rearrange("p (t c) -> p t c", c=P),
                                                 ACT.Copy).then_inc(sem("aux_used"), 1)
                            aux += 1
            act.wait_ge(sem("silu"), NM)
            for zb in range(2 * NL):
                act.wait_ge(sem("zps"), zb + 1)
                if zb >= 2:
                    act.wait_ge(sem(f"z_out{zb % 2}"), 16 * (zb // 2))
                nc.scalar.activation(zst[zb % 2], zbank[zb % 4][:], ACT.Silu).then_inc(sem("zsb"), 1)
                act.wait_ge(sem("zsb"), zb + 1)
                act.dma_start(z_dram[zb % NL, :, (zb // NL) * 512:(zb // NL + 1) * 512], zst[zb % 2])\
                    .then_inc(sem(f"z_out{zb % 2}"), 16)
            act_scan(act)
            act_tail(act)

        @block.vector
        def _(dve):
            chain = [0]

            def link(ins):
                chain[0] += 1
                ins.then_inc(sem("dve_chain"), 1)
                dve.wait_ge(sem("dve_chain"), chain[0])

            v = nc.vector
            v.memset(eps_d[:], EPS)
            v.memset(eps1[:], EPS)
            v.memset(eps_q[:], EPS * DK)
            for i in range(2):
                v.memset(cin_l[i], 0.0).then_inc(sem("pad"), 1)
                v.memset(cin_c[i], 0.0).then_inc(sem("pad"), 1)
            dve.wait_ge(sem("vT"), 2)
            v.tensor_copy(vcols[:], ps[0][:, 0:NV]).then_inc(sem("vcols"), 1)
            v.tensor_copy(sbc[:], ps[1][:, 0:56]).then_inc(sem("vcols"), 1)
            for b in range(NAB):
                dve.wait_ge(sem("ada_used"), b + 1)
                v.tensor_copy(mrow[:, b * 512:(b + 1) * 512], ps[2 + b % 2][0:2, :]).then_inc(sem("mrow"), 1)
            dve.wait_ge(sem("vcols"), 2)
            dve.wait_ge(sem("vT"), 3)
            link(v.tensor_tensor(mods[:, 0:2 * KD, :], ps[1][:, 0:4 * KD].rearrange("p (j w) -> p j w", w=2),
                                 vcols[:, V_AB:V_AB + 2 * KD].unsqueeze(2).to_broadcast([P, 2 * KD, 2]), ALU.add))
            v.scalar_tensor_tensor(gain1[:], mods[:, KD:2 * KD, :], 1.0,
                                   vcols[:, V_NG:V_NG + KD].unsqueeze(2).to_broadcast([P, KD, 2]),
                                   ALU.add, ALU.mult).then_inc(sem("gain1"), 1)
            for t in range(NT):
                dve.wait_ge(sem("rms"), t + 1)
                link(v.reciprocal(rstd[:, t:t + 1], rstd[:, t:t + 1]))
                v.tensor_scalar(xall[:, t, :], xall[:, t, :], rstd[:, t:t + 1], None, ALU.mult)\
                    .then_inc(sem("xn"), 1)
            dve.wait_ge(sem("Gps"), 1)
            v.tensor_copy(gates[:], ps[7][:, 0:NT * NGATE].rearrange("p (t g) -> p t g", g=NGATE))\
                .then_inc(sem("graw"), 1)
            dve.wait_ge(sem("graw"), 2)
            v.scalar_tensor_tensor(beta_f, gates[:, :, 0:2 * DN_H], -1.0, gates[:, :, 0:2 * DN_H],
                                   ALU.mult, ALU.min).then_inc(sem("gabs"), 1)
            for d in range(2):
                a0, t0 = 2 * DN_H + d * DN_H, 4 * DN_H + d * SSM_H
                for g0, n, c0 in ((0, DN_H, a0), (DN_H, SSM_H, t0)):
                    ins = v.tensor_tensor(ga[:, :, d, g0:g0 + n], gates[:, :, c0:c0 + n],
                                          sbc[:, d * GD + g0:d * GD + g0 + n].unsqueeze(1).to_broadcast([P, NT, n]),
                                          ALU.add)
            link(ins)
            gaf, gbf, Gf, eGf, eGtf, spf = (a[:].rearrange("p t d g -> p (t d g)") for a in (ga, gb, G, eG, eGt, sp))
            v.scalar_tensor_tensor(gbf, gaf, -1.0, gaf, ALU.mult, ALU.min).then_inc(sem("gabs"), 1)
            dve.wait_ge(sem("gexp"), 3)
            link(v.scalar_tensor_tensor(gates[:, :, 0:2 * DN_H], gates[:, :, 0:2 * DN_H], 0.0, beta_f,
                                        ALU.is_ge, ALU.max))
            link(v.tensor_scalar(beta_f, beta_f, 1.0, None, ALU.add))
            link(v.reciprocal(beta_f, beta_f))
            link(v.tensor_tensor(beta_f, beta_f, gates[:, :, 0:2 * DN_H], ALU.mult))
            v.tensor_scalar(Gf, gbf, 1.0, None, ALU.add).then_inc(sem("gln"), 1)
            dve.wait_ge(sem("gln_out"), 1)
            link(v.tensor_scalar(Gf, Gf, -1.0, None, ALU.add))
            link(v.tensor_scalar(eGtf, Gf, 0.0, None, ALU.is_equal))
            v.tensor_tensor(Gf, Gf, eGtf, ALU.add)
            link(v.tensor_tensor(eGf, eGf, eGtf, ALU.add))
            link(v.reciprocal(Gf, Gf))
            link(v.tensor_tensor(Gf, Gf, eGf, ALU.mult))
            link(v.tensor_tensor(Gf, Gf, gbf, ALU.mult))
            link(v.scalar_tensor_tensor(spf, gaf, 0.0, Gf, ALU.max, ALU.add))
            v.scalar_tensor_tensor(ga[:].rearrange("p t d g -> p t (d g)"), sp[:].rearrange("p t d g -> p t (d g)"),
                                   -1.0, gneg[:].rearrange("p d g -> p (d g)").unsqueeze(1)
                                   .to_broadcast([P, NT, 2 * GD]), ALU.mult, ALU.mult).then_inc(sem("logg"), 1)
            dve.wait_ge(sem("Gps"), 2)
            v.tensor_copy(G[:], ps[7][:, 0:240].rearrange("p (d t g) -> p t d g", d=2, g=GD)).then_inc(sem("Gev"), 1)
            v.tensor_copy(gbf, ps[7][:, 240:480]).then_inc(sem("Gev"), 1)
            dve.wait_ge(sem("Gev"), 2)
            v.tensor_tensor(gaf, gbf, Gf, ALU.subtract).then_inc(sem("Gev"), 1)
            dve.wait_ge(sem("eG"), 3)
            v.tensor_tensor(wtail[:, :, :, 0:DN_H], wtail[:, :, :, 0:DN_H], beta[:], ALU.mult).then_inc(sem("wtail"), 1)
            v.tensor_tensor(wtail[:, :, :, DN_H:GD], wtail[:, :, :, DN_H:GD], sp[:, :, :, DN_H:GD], ALU.mult)\
                .then_inc(sem("wtail"), 1)

            dve.wait_ge(sem("taps_in"), 32)
            assert tiles[NM - 1][1] == "C"
            for m in range(NM):
                col, kind, i, has_ctx = tiles[m]
                tp = taps[:, col // P, :]
                acc = cacc[m % 2]
                accg = acc[:, 0:T].rearrange("p (r c) -> p r c", c=GW)
                dve.wait_ge(sem("cin"), m + 1)
                if m >= 2:
                    dve.wait_ge(sem("silu"), m - 1)
                if has_ctx:
                    link(v.tensor_scalar(acc[:, T:TA], cin_c[m % 2][:, 0:TC], tp[:, 3:4], None, ALU.mult))
                    for j in (1, 2):
                        link(v.scalar_tensor_tensor(acc[:, T:TA], cin_c[m % 2][:, j:j + TC], tp[:, 3 + j:4 + j],
                                                    acc[:, T:TA], ALU.mult, ALU.add))
                link(v.tensor_scalar(accg, cin_l[m % 2][:, 0:GR, 0:GW], tp[:, 0:1], None, ALU.mult))
                for j in range(1, 9):
                    ins = v.scalar_tensor_tensor(accg, cin_l[m % 2][:, j // 3:j // 3 + GR, j % 3:j % 3 + GW],
                                                 tp[:, j:j + 1], accg, ALU.mult, ALU.add)
                    if j < 8:
                        link(ins)
                    if j == 4 and m >= 1 and tiles[m - 1][1] in "kq":
                        w = TA if tiles[m - 1][3] else T
                        dve.wait_ge(sem("aux_used"), n_aux(m))
                        v.reciprocal(ctmp[:, 0:w], ctmp[:, 0:w]).then_inc(sem("nrm_rec"), 1)
                ins.then_inc(sem("conv"), 1)
                b = m - LATE + 2
                if 0 <= b < NLB:
                    blk = lring[b % 2]
                    dve.wait_ge(sem(f"late_in{b % 2}"), 16 * (b // 2 + 1))
                    link(v.tensor_scalar(blk[:, 0, :], blk[:, 0, :], silu_c[:, 0, 0:1], None, ALU.mult))
                    for k in range(1, KD):
                        ins = v.scalar_tensor_tensor(blk[:, 0, :], blk[:, k, :], silu_c[:, k, 0:1], blk[:, 0, :],
                                                     ALU.mult, ALU.add)
                        if k < KD - 1:
                            link(ins)
                    ins.then_inc(sem("late"), 1)
            dve.wait_ge(sem("nrm_mul"), 2 * DN_H)
            dve.wait_ge(sem("aux_used"), n_aux(NM))
            dve.wait_ge(sem("wtail"), 2)
            for d in range(2):
                for q, g0, n, src in ((Q_G, 0, GD, G), (Q_EG, 0, GD, eG), (Q_EGT, 0, GD, eGt), (Q_WT, 0, GD, wtail),
                                      (Q_W, 0, DN_H, beta)):
                    v.tensor_copy(pack[:, :, d, q, g0:g0 + n], src[:, :, d, :])
                v.tensor_copy(pack[:, :, d, Q_W, DN_H:GD], sp[:, :, d, SM]).then_inc(sem("pack"), 1)
            dve_scan(dve, link)
            dve_tail(dve, link)


def kernel(**inputs):
    import concourse.bacc as bacc
    import numpy as np
    from concourse.bass_utils import run_bass_kernel_spmd

    names = ["x", "c", "ctx", "c_ctx", "ada_w", "ada_b", "norm_g", "w_in", "conv_w", "conv_b", "dn_A_log",
             "dn_dt_bias", "dn_norm_g", "ssm_A_log", "ssm_dt_bias", "ssm_D", "ssm_norm_g", "w_out", "router_w",
             "exp_w_gate", "exp_w_up", "exp_w_down"]
    nc = bacc.Bacc("TRN2", target_bir_lowering=False, num_devices=1)
    arrays = {n: np.ascontiguousarray(inputs[n]) for n in names}
    args = [nc.dram_tensor(n, arrays[n].shape, mybir.dt.from_np(arrays[n].dtype), kind="ExternalInput").ap()
            for n in names]
    out = nc.dram_tensor("out", arrays["x"].shape, F32, kind="ExternalOutput").ap()
    hybrid_block(nc, *args, out)
    r = run_bass_kernel_spmd(nc, [arrays], core_ids=[0])
    return r.results[0]["out"]
```
